# Optimizing a Trainium2 kernel written in Bass

```python
import math
import numpy as np
import jax
import jax.numpy as jnp
from jax import lax

D_MODEL = 2048
BATCH = 1
SEQ = 256
DEPTH = 1

N_MIXERS = 2
GM_WIDTH = D_MODEL
GM_GROUPS = 8
GM_GROUP_DIM = GM_WIDTH // GM_GROUPS
GM_CHUNK = 128
NSA_HEAD_DIM = 128
NSA_HEADS = D_MODEL // NSA_HEAD_DIM
NSA_KV_HEADS = 4
NSA_GQA = NSA_HEADS // NSA_KV_HEADS
CMP_LEN = 32
CMP_STRIDE = 16
SEL_BLK = 64
SEL_TOPN = 16
SEL_LOCAL = 2
WINDOW = 512
Q_BLK = 128
FORCE = 1.0e4
NSA_Q_DIM = NSA_HEADS * NSA_HEAD_DIM
NSA_KV_DIM = NSA_KV_HEADS * NSA_HEAD_DIM
NSA_IN_DIM = NSA_Q_DIM + 6 * NSA_KV_DIM + 3 * NSA_HEADS
N_GROUPS = 4
EXP_PER_GROUP = 8
N_EXPERTS = N_GROUPS * EXP_PER_GROUP
TOP_K = 2
D_EXPERT = 512
MOE_BLK = 256
EPS = 1e-6
NEG = -1e30

kernel_name = "hybrid_gmlp_nsa_hmoe"

def rmsnorm(x, g):
    xf = x.astype(jnp.float32)
    y = xf * lax.rsqrt(jnp.mean(xf * xf, axis=-1, keepdims=True) + EPS)
    return (y * g.astype(jnp.float32)).astype(x.dtype)

def layernorm(x, g, b):
    xf = x.astype(jnp.float32)
    mu = jnp.mean(xf, axis=-1, keepdims=True)
    xc = xf - mu
    y = xc * lax.rsqrt(jnp.mean(xc * xc, axis=-1, keepdims=True) + EPS)
    return (y * g.astype(jnp.float32) + b.astype(jnp.float32)).astype(x.dtype)

def masked_softmax(s, mask):
    s = jnp.where(mask, s.astype(jnp.float32), NEG)
    m = jnp.max(s, axis=-1, keepdims=True)
    p = jnp.where(mask, jnp.exp(s - m), 0.0)
    return p / jnp.maximum(jnp.sum(p, axis=-1, keepdims=True), 1e-30)

def chunked_gmlp(h, w_in, ln_g, ln_b, w_s, b_s, w_out):
    B, S, _ = h.shape
    z = jax.nn.gelu(h @ w_in)
    u, v = jnp.split(z, 2, axis=-1)
    v = layernorm(v, ln_g, ln_b)
    v = v.reshape(B, S // GM_CHUNK, GM_CHUNK, GM_GROUPS, GM_GROUP_DIM)
    causal = jnp.tril(jnp.ones((GM_CHUNK, GM_CHUNK), dtype=w_s.dtype))
    sv = jnp.einsum('gts,bcsgd->bctgd', w_s * causal, v) + b_s.T[None, None, :, :, None]
    y = u * sv.reshape(B, S, GM_WIDTH)
    return y @ w_out

def compress_kv(k, pe, w1, w2):
    B, S, Hk, Dh = k.shape
    n_c = (S - CMP_LEN) // CMP_STRIDE + 1
    idx = np.arange(n_c)[:, None] * CMP_STRIDE + np.arange(CMP_LEN)[None, :]
    blocks = k[:, idx] + pe[None, None, :, None, :]
    flat = blocks.transpose(0, 1, 3, 2, 4).reshape(B, n_c, Hk, CMP_LEN * Dh)
    return jax.nn.gelu(flat @ w1) @ w2

def nsa_attention(h, w_in, ck_pe, ck_w1, ck_w2, cv_pe, cv_w1, cv_w2, w_out):
    B, S, _ = h.shape
    Hk, G, Dh = NSA_KV_HEADS, NSA_GQA, NSA_HEAD_DIM
    proj = h @ w_in
    splits = [NSA_Q_DIM + i * NSA_KV_DIM for i in range(7)]
    q, k_c, v_c, k_s, v_s, k_w, v_w, g = jnp.split(proj, splits, axis=-1)
    q = q.reshape(B, S, Hk, G, Dh) * (Dh ** -0.5)
    kv = lambda a: a.reshape(B, S, Hk, Dh)
    gates = jax.nn.sigmoid(g.astype(jnp.float32)).reshape(B, S, Hk, G, 3).astype(h.dtype)

    kc = compress_kv(kv(k_c), ck_pe, ck_w1, ck_w2)
    vc = compress_kv(kv(v_c), cv_pe, cv_w1, cv_w2)
    n_c = kc.shape[1]
    cmp_end = jnp.asarray(np.arange(n_c) * CMP_STRIDE + CMP_LEN - 1)
    n_sel = S // SEL_BLK
    n_top = min(SEL_TOPN, n_sel)
    ci = np.arange(n_c)[:, None] * CMP_STRIDE
    sj = np.arange(n_sel)[None, :] * SEL_BLK
    overlap = jnp.asarray(((ci < sj + SEL_BLK) & (ci + CMP_LEN > sj)).astype(np.float32))

    ks_blk = kv(k_s).reshape(B, n_sel, SEL_BLK, Hk, Dh).transpose(0, 3, 1, 2, 4)
    vs_blk = kv(v_s).reshape(B, n_sel, SEL_BLK, Hk, Dh).transpose(0, 3, 1, 2, 4)
    kw_pad = jnp.pad(kv(k_w), ((0, 0), (WINDOW, 0), (0, 0), (0, 0)))
    vw_pad = jnp.pad(kv(v_w), ((0, 0), (WINDOW, 0), (0, 0), (0, 0)))
    gather = jax.vmap(jax.vmap(lambda blocks, idx: blocks[idx]))
    blk = jnp.arange(n_sel)

    def query_block(qb):
        q0 = qb * Q_BLK
        t = q0 + jnp.arange(Q_BLK)
        qblk = lax.dynamic_slice_in_dim(q, q0, Q_BLK, axis=1)
        gblk = lax.dynamic_slice_in_dim(gates, q0, Q_BLK, axis=1)
        mask_c = cmp_end[None, :] <= t[:, None]
        p_c = masked_softmax(jnp.einsum('bqhgd,bchd->bhgqc', qblk, kc), mask_c)
        o_c = jnp.einsum('bhgqc,bchd->bqhgd', p_c.astype(vc.dtype), vc)
        imp = jnp.einsum('bhgqc,cj->bhqj', p_c, overlap)
        cur = (t // SEL_BLK)[:, None]
        valid = blk[None, :] * SEL_BLK <= t[:, None]
        dist = cur - blk[None, :]
        forced = (blk[None, :] == 0) | ((dist >= 0) & (dist < SEL_LOCAL))
        score = jnp.where(valid, jnp.where(forced, FORCE, imp), NEG)
        _, top_idx = lax.top_k(score, n_top)
        k_sel = gather(ks_blk, top_idx).reshape(B, Hk, Q_BLK, n_top * SEL_BLK, Dh)
        v_sel = gather(vs_blk, top_idx).reshape(B, Hk, Q_BLK, n_top * SEL_BLK, Dh)
        pos_s = (top_idx[..., None] * SEL_BLK + jnp.arange(SEL_BLK)).reshape(B, Hk, Q_BLK, n_top * SEL_BLK)
        mask_s = (pos_s <= t[:, None])[:, :, None]
        p_s = masked_softmax(jnp.einsum('bqhgd,bhqkd->bhgqk', qblk, k_sel), mask_s)
        o_s = jnp.einsum('bhgqk,bhqkd->bqhgd', p_s.astype(v_sel.dtype), v_sel)
        k_win = lax.dynamic_slice_in_dim(kw_pad, q0, WINDOW + Q_BLK, axis=1)
        v_win = lax.dynamic_slice_in_dim(vw_pad, q0, WINDOW + Q_BLK, axis=1)
        pos_w = q0 - WINDOW + jnp.arange(WINDOW + Q_BLK)
        mask_w = (pos_w[None, :] <= t[:, None]) & (pos_w[None, :] > t[:, None] - WINDOW) & (pos_w[None, :] >= 0)
        p_w = masked_softmax(jnp.einsum('bqhgd,bkhd->bhgqk', qblk, k_win), mask_w)
        o_w = jnp.einsum('bhgqk,bkhd->bqhgd', p_w.astype(v_win.dtype), v_win)
        o = gblk[..., 0:1] * o_c + gblk[..., 1:2] * o_s + gblk[..., 2:3] * o_w
        return o.reshape(B, Q_BLK, NSA_Q_DIM)

    o = lax.map(query_block, jnp.arange(S // Q_BLK))
    o = o.transpose(1, 0, 2, 3).reshape(B, S, NSA_Q_DIM)
    return o @ w_out

def hier_moe(h, w_group, b_group, w_exp, b_exp, w_gate, w_up, w_down):
    B, S, D = h.shape
    T = B * S
    xt = h.reshape(T, D)
    g_prob = jax.nn.softmax((xt @ w_group).astype(jnp.float32) + b_group.astype(jnp.float32), axis=-1)
    g_w, g_idx = lax.top_k(g_prob, 1)
    e_logits = ((xt @ w_exp).astype(jnp.float32) + b_exp.astype(jnp.float32)).reshape(T, N_GROUPS, EXP_PER_GROUP)
    e_logits = jnp.take_along_axis(e_logits, g_idx[:, :, None], axis=1)[:, 0]
    e_w, e_idx = lax.top_k(jax.nn.softmax(e_logits, axis=-1), TOP_K)
    e_w = e_w / jnp.sum(e_w, axis=-1, keepdims=True)
    weight = (g_w * e_w).reshape(-1)
    expert = (g_idx * EXP_PER_GROUP + e_idx).reshape(-1).astype(jnp.int32)
    token = jnp.repeat(jnp.arange(T, dtype=jnp.int32), TOP_K)
    n_assign = T * TOP_K
    order = jnp.argsort(expert)
    s_exp, s_tok, s_w = expert[order], token[order], weight[order]
    counts = jnp.bincount(expert, length=N_EXPERTS)
    padded = (counts + MOE_BLK - 1) // MOE_BLK * MOE_BLK
    pad_end = jnp.cumsum(padded)
    pad_start = pad_end - padded
    start = jnp.cumsum(counts) - counts
    dest = pad_start[s_exp] + jnp.arange(n_assign, dtype=jnp.int32) - start[s_exp]
    n_rows = (n_assign + MOE_BLK - 1) // MOE_BLK * MOE_BLK + N_EXPERTS * MOE_BLK
    n_blocks = n_rows // MOE_BLK
    row_tok = jnp.full((n_rows,), T, jnp.int32).at[dest].set(s_tok)
    row_w = jnp.zeros((n_rows,), jnp.float32).at[dest].set(s_w)
    block_exp = jnp.minimum(jnp.searchsorted(pad_end, jnp.arange(n_blocks) * MOE_BLK, side='right'),
                            N_EXPERTS - 1)
    x_pad = jnp.concatenate([xt, jnp.zeros((1, D), xt.dtype)], axis=0)

    def run_block(args):
        rows, e = args
        xb = x_pad[rows]
        return (jax.nn.silu(xb @ w_gate[e]) * (xb @ w_up[e])) @ w_down[e]

    y = lax.map(run_block, (row_tok.reshape(n_blocks, MOE_BLK), block_exp))
    y = y.reshape(n_rows, D) * row_w[:, None].astype(y.dtype)
    out = jnp.zeros((T + 1, D), y.dtype).at[row_tok].add(y)[:T]
    return out.reshape(B, S, D)

def setup_inputs(seed: int = 0) -> dict:
    key = jax.random.key(seed)
    keys = list(jax.random.split(key, 32))

    def nrm(shape, scale):
        return jax.random.normal(keys.pop(), shape, jnp.float32) * scale

    n_a = (DEPTH + N_MIXERS - 1) // N_MIXERS
    n_b = DEPTH // N_MIXERS
    Dh = NSA_HEAD_DIM
    return {
        "x": nrm((BATCH, SEQ, D_MODEL), 1.0),
        "norm_mix": 1.0 + nrm((DEPTH, D_MODEL), 0.02),
        "norm_ffn": 1.0 + nrm((DEPTH, D_MODEL), 0.02),
        "norm_final": 1.0 + nrm((D_MODEL,), 0.02),
        "a_w_in": nrm((n_a, D_MODEL, 2 * GM_WIDTH), D_MODEL ** -0.5),
        "a_ln_g": 1.0 + nrm((n_a, GM_WIDTH), 0.02),
        "a_ln_b": nrm((n_a, GM_WIDTH), 0.02),
        "a_w_s": nrm((n_a, GM_GROUPS, GM_CHUNK, GM_CHUNK), GM_CHUNK ** -0.5),
        "a_b_s": 1.0 + nrm((n_a, GM_GROUPS, GM_CHUNK), 0.02),
        "a_w_out": nrm((n_a, GM_WIDTH, D_MODEL), GM_WIDTH ** -0.5),
        "b_w_in": nrm((n_b, D_MODEL, NSA_IN_DIM), D_MODEL ** -0.5),
        "b_ck_pe": nrm((n_b, CMP_LEN, Dh), 0.1),
        "b_ck_w1": nrm((n_b, CMP_LEN * Dh, Dh), (CMP_LEN * Dh) ** -0.5),
        "b_ck_w2": nrm((n_b, Dh, Dh), Dh ** -0.5),
        "b_cv_pe": nrm((n_b, CMP_LEN, Dh), 0.1),
        "b_cv_w1": nrm((n_b, CMP_LEN * Dh, Dh), (CMP_LEN * Dh) ** -0.5),
        "b_cv_w2": nrm((n_b, Dh, Dh), Dh ** -0.5),
        "b_w_out": nrm((n_b, NSA_Q_DIM, D_MODEL), NSA_Q_DIM ** -0.5),
        "r_w_group": nrm((DEPTH, D_MODEL, N_GROUPS), D_MODEL ** -0.5),
        "r_b_group": nrm((DEPTH, N_GROUPS), 0.01),
        "r_w_exp": nrm((DEPTH, D_MODEL, N_EXPERTS), D_MODEL ** -0.5),
        "r_b_exp": nrm((DEPTH, N_EXPERTS), 0.01),
        "e_w_gate": nrm((DEPTH, N_EXPERTS, D_MODEL, D_EXPERT), D_MODEL ** -0.5),
        "e_w_up": nrm((DEPTH, N_EXPERTS, D_MODEL, D_EXPERT), D_MODEL ** -0.5),
        "e_w_down": nrm((DEPTH, N_EXPERTS, D_EXPERT, D_MODEL), D_EXPERT ** -0.5),
    }

def reference(x, norm_mix, norm_ffn, norm_final, a_w_in, a_ln_g, a_ln_b, a_w_s, a_b_s, a_w_out,
              b_w_in, b_ck_pe, b_ck_w1, b_ck_w2, b_cv_pe, b_cv_w1, b_cv_w2, b_w_out,
              r_w_group, r_b_group, r_w_exp, r_b_exp, e_w_gate, e_w_up, e_w_down):
    h = x
    for i in range(DEPTH):
        hn = rmsnorm(h, norm_mix[i])
        j = i // N_MIXERS
        if i % N_MIXERS == 0:
            mix = chunked_gmlp(hn, a_w_in[j], a_ln_g[j], a_ln_b[j], a_w_s[j], a_b_s[j], a_w_out[j])
        else:
            mix = nsa_attention(hn, b_w_in[j], b_ck_pe[j], b_ck_w1[j], b_ck_w2[j],
                                b_cv_pe[j], b_cv_w1[j], b_cv_w2[j], b_w_out[j])
        h = h + mix
        h = h + hier_moe(rmsnorm(h, norm_ffn[i]), r_w_group[i], r_b_group[i], r_w_exp[i], r_b_exp[i],
                         e_w_gate[i], e_w_up[i], e_w_down[i])
    return rmsnorm(h, norm_final)


_drawn_inputs = setup_inputs


def setup_inputs(seed=0):
    import zlib

    import numpy as np

    out = dict(_drawn_inputs(seed))
    spreads = {}
    factors = {'norm_final': 7.455,
     'a_ln_g': 20.812,
     'a_ln_b': 18.211,
     'a_b_s': 10.853,
     'r_b_group': 20.909,
     'r_b_exp': 16.46,
     'norm_ffn': 6.285}
    for name, (base, spread) in spreads.items():
        noise = np.random.default_rng([zlib.crc32(name.encode()), seed]).standard_normal(out[name].shape)
        drawn = base * np.exp(spread * noise) if base else spread * noise
        out[name] = jnp.asarray(drawn.astype(out[name].dtype))
    for name, factor in factors.items():
        out[name] = (out[name] * factor).astype(out[name].dtype)
    return out
```

```python
from contextlib import ExitStack

import concourse.bass as bass
from concourse import mybir

F32 = mybir.dt.float32
F32R = mybir.dt.float32r
I32 = mybir.dt.int32
ALU = mybir.AluOpType
ACT = mybir.ActivationFunctionType
AX_X = mybir.AxisListType.X

P = 128
EPS = 1e-6
CAP = 32
BIG = 1.0e30


def hybrid_layer(nc, x, norm_mix, norm_ffn, norm_final, w_in, ln_g, ln_b, w_s, b_s, w_out,
                 r_w_group, r_b_group, r_w_exp, r_b_exp, e_gate, e_up, e_down, out):
    _, T, D = x.shape
    NT = T // P
    KD = D // P
    NBLK = 512
    NB = D // NBLK
    GRP = w_s.shape[1]
    GD = D // GRP
    NGRP = r_w_group.shape[2]
    NEXP = r_w_exp.shape[2]
    EPG = NEXP // NGRP
    NR = NGRP + NEXP
    FE = e_gate.shape[3]
    FT = FE // P
    NC = 12
    KC = 4
    HC = 8
    NQ = P // CAP
    MAXP = T // CAP
    assert (NT, KD, NB, FT, NQ, GD, NGRP * EPG) == (2, 16, 4, 4, 4, 256, NEXP)

    with ExitStack() as ctx:
        def sem(name):
            return ctx.enter_context(nc.semaphore(name))

        def sb(name, shape, dt=F32, stack=ctx):
            return stack.enter_context(nc.sbuf_tensor(name, shape, dt))

        ring = sb("ring", [P, NC, 2048])
        h = sb("h", [P, NT, D])
        v = sb("v", [P, NT, D])
        ident = sb("ident", [P, P])
        iota_cap = sb("iota_cap", [P, P])
        iota_pass = sb("iota_pass", [P, P])
        before = sb("before", [P, P])
        ones = sb("ones", [P, P])
        w_router = sb("w_router", [P, KD, NR])
        b_router = sb("b_router", [P, NR])
        col_rows = sb("col_rows", [2 * KD + GRP, P])
        cols_T = sb("cols_T", [P, 2 * KD + GRP])
        g_mix, g_ffn, bias_s = cols_T[:, 0:KD], cols_T[:, KD:2 * KD], cols_T[:, 2 * KD:2 * KD + GRP]
        v_stats = sb("v_stats", [P, NT, NB, 6])
        v_mean_var = sb("v_mean_var", [P, NT, 2])
        rows = sb("rows", [P, 12, NT])
        sumsq_h = sb("sumsq_h", [P, NT, NB])
        eps_col = sb("eps_col", [P, 1])
        iota_e = sb("iota_e", [P, NEXP])
        rank_of = sb("rank_of", [P, NT, NEXP])
        weight_of = sb("weight_of", [P, NT, NEXP])
        count_i = sb("count_i", [P, NEXP], I32)
        extra_i = sb("extra_i", [P, NEXP], I32)
        extra_before_i = sb("extra_before_i", [P, NEXP], I32)
        rstd_x, rms_x, ssq_x, rstd_v, std_v = (rows[:, i, :] for i in range(5))
        rstd_h, rms_h, ssq_h, rstd_o, rms_o, ssq_o = (rows[:, i, :] for i in range(5, 11))

        with ExitStack() as mixer:
            xT_hi = sb("xT_hi", [P, KD, T], F32R, mixer)
            xT_lo = sb("xT_lo", [P, KD, T], F32R, mixer)
            w_raw = sb("w_raw", [P, 4, 2, NBLK], F32, mixer)
            w_hi = sb("w_hi", [P, 2, 2, NBLK], F32R, mixer)
            w_lo = sb("w_lo", [P, 2, 2, NBLK], F32R, mixer)
            u = sb("u", [P, 2, NT, NBLK], F32, mixer)
        acc = sb("acc", [P, NT, D])
        g_final = sb("g_final", [P, D])
        xeT = sb("xeT", [P, KD, CAP])
        gu = sb("gu", [P, 256])
        silu_g = sb("silu_g", [P, 2, 2 * CAP])
        hT = sb("hT", [P, 2, 2 * CAP])
        y = sb("y", [P, NBLK])
        scatT = sb("scatT", [P, NT, P])
        scat = sb("scat", [P, NT, P])
        sel = sb("sel", [P, NT, CAP])
        lg = sb("lg", [P, NT, NR])
        rt = sb("rt", [P, 12, NT, NEXP])
        rc = sb("rc", [P, 8, NT])

        ws_raw = ring[:, 9, 0:GRP * P].rearrange("p (g s) -> p g s", g=GRP)
        ws_T = ring[:, 9, GRP * P:2 * GRP * P].rearrange("p (g s) -> p g s", g=GRP)
        g_ln, b_ln = ring[:, 10, :], ring[:, 11, :]
        hgT = v[:, :, :].rearrange("p a (b t) -> p (a b) t", t=T)

        bank = [ctx.enter_context(nc.psum_tensor(f"bank{i}", [P, NBLK], F32)) for i in range(8)]
        Z = [[bank[0], bank[1]], [bank[2], bank[3]]]
        X = [bank[4], bank[5]]
        L = bank[6]
        R = bank[7]
        O = [bank[0], bank[1], bank[2], bank[3]]
        G, GU, TR, Y = bank[4], bank[5], bank[6], bank[7]

        x_in = [sem(f"x_in{t}") for t in range(NT)]
        raw_in = [sem(f"raw_in{s}") for s in range(4)]
        chunk_in = [sem(f"chunk_in{c}") for c in range(NC)]
        cols_in, cols_ps, cols_done = sem("cols_in"), sem("cols_ps"), sem("cols_done")
        ws_in, router_in, ln_in, final_in = sem("ws_in"), sem("router_in"), sem("ln_in"), sem("final_in")
        consts, ws_masked = sem("consts"), sem("ws_masked")
        xt_ps, xt_hi, xt_lo = sem("xt_ps"), sem("xt_hi"), sem("xt_lo")
        hi_done, lo_done, w_used = sem("hi_done"), sem("lo_done"), sem("w_used")
        v_ready, u_ready, y_done = sem("v_ready"), sem("u_ready"), sem("y_done")
        ln_step, ln_done, var_done, std_done = sem("ln_step"), sem("ln_done"), sem("var_done"), sem("std_done")
        wst_ps, wst_done = sem("wst_ps"), sem("wst_done")
        sv_ps, sv_done = sem("sv_ps"), sem("sv_done")
        yt_ps, yt_hi, yt_lo = sem("yt_ps"), sem("yt_hi"), sem("yt_lo")
        sumsq_x_done, rms_x_done, rstd_x_done = sem("sumsq_x_done"), sem("rms_x_done"), sem("rstd_x_done")
        h_done, sumsq_h_done = sem("h_done"), sem("sumsq_h_done")
        ht_ps, ht_done = sem("ht_ps"), sem("ht_done")
        ssq_h_done, rms_h_done = sem("ssq_h_done"), sem("rms_h_done")
        logits_ps, mask_done, ranks_ps, exp_in, exp_done = (
            sem("logits_ps"), sem("mask_done"), sem("ranks_ps"), sem("exp_in"), sem("exp_done"))
        r_step, counts_ready, extra_ready, p_step = (
            sem("r_step"), sem("counts_ready"), sem("extra_ready"), sem("p_step"))
        acc_init = sem("acc_init")
        extras_over = sem("extras_over")
        chunk_used, no_more_passes = sem("chunk_used"), sem("no_more_passes")
        ssq_o_done, rms_o_done, rstd_o_done, out_ready, out_stored = (
            sem("ssq_o_done"), sem("rms_o_done"), sem("rstd_o_done"), sem("out_ready"), sem("out_stored"))

        class PassSems:

            def __init__(self, s):
                self.sel = sem(f"sel_ready{s}")
                self.scat = sem(f"scat_ready{s}")
                self.gathered = sem(f"gathered{s}")
                self.xe = sem(f"xe_ready{s}")
                self.scat_ps = sem(f"scat_ps{s}")
                self.scatT = sem(f"scatT_ready{s}")
                self.gu_ps = sem(f"gu_ps{s}")
                self.gu = sem(f"gu_ready{s}")
                self.tr_ps = sem(f"tr_ps{s}")
                self.silu = sem(f"silu_ready{s}")
                self.hT = sem(f"hT_ready{s}")
                self.y_ps = sem(f"y_ps{s}")
                self.y = sem(f"y_ready{s}")
                self.scattered = sem(f"scattered{s}")
                self.o_free = sem(f"o_free{s}")

        first, extra = PassSems(""), PassSems("_x")

        def adds_done(n_passes):
            return n_passes * NT * NB + NB

        def w_in_half(col, hc):
            return w_in[0, hc * 2 * P:(hc + 1) * 2 * P, bass.ds(col, NBLK)].rearrange("(j p) n -> p j n", p=P)

        def w_out_half(col, hc):
            return w_out[0, hc * 2 * P:(hc + 1) * 2 * P, col:col + NBLK].rearrange("(j p) n -> p j n", p=P)

        def expert_chunk(e, c):
            if c < 8:
                w, k = (e_gate, e_up)[c % 2], c // 2
                return w[0, e, k * KC * P:(k + 1) * KC * P, :].rearrange("(j p) n -> p j n", p=P)
            return e_down[0, e, (c - 8) * P:(c - 7) * P, :]

        def ring_slot(c):
            return ring[:, c, :].rearrange("p (j n) -> p j n", j=KC) if c < 8 else ring[:, c, :]

        def experts(eng, run_pass, after_extra, at_start=None):
            with eng.Fori(0, NEXP) as e:
                count = eng.value_load(count_i[0:1, bass.ds(e, 1)], min_val=0, max_val=T)
                if at_start is not None:
                    with eng.If(count <= CAP):
                        at_start()
                    with eng.Else():
                        eng.nop()
                run_pass(first, e)
                with eng.If(count > CAP):
                    eng.wait_ge(extra_ready, 1)
                    eng.wait_ge(first.o_free, adds_done(e + 1))
                    n_extra = eng.value_load(extra_i[0:1, bass.ds(e, 1)], min_val=1, max_val=MAXP - 1)
                    n_before = eng.value_load(extra_before_i[0:1, bass.ds(e, 1)], min_val=0, max_val=T * 2 // CAP)
                    with eng.Fori(0, n_extra) as q:
                        run_pass(extra, n_before + q)
                    eng.wait_ge(extra.o_free, adds_done(n_before + n_extra))
                    after_extra()
                with eng.Else():
                    eng.nop()

        block = ctx.enter_context(nc.Block())

        @block.sync
        def _(sp):
            for t in range(NT):
                sp.dma_start(h[:, t, :], x[0, t * P:(t + 1) * P, :]).then_inc(x_in[t], 16)

            def load_half(src, n, hc, first_block=False):
                if not (first_block and hc < 4):
                    sp.wait_ge(lo_done, HC * n + hc - 3)
                sp.dma_start(w_raw[:, hc % 4, :, :], src).then_inc(raw_in[hc % 4], 16)

            def load_first_expert(c):
                sp.dma_start(ring_slot(c), expert_chunk(0, c)).then_inc(chunk_in[c], 16)

            for n in range(2 * NB):
                col = D + n * NBLK if n < NB else (n - NB) * NBLK
                for hc in range(HC):
                    load_half(w_in_half(col, hc), n, hc, n == 0)
                load_first_expert(n)
            for n in range(NB):
                for hc in range(HC):
                    load_half(w_out_half(n * NBLK, hc), 2 * NB + n, hc)
                c = 2 * NB + n
                if c == 9:
                    sp.wait_ge(sv_ps, NT * GRP // 2)
                if c == 10:
                    sp.wait_ge(ln_done, NT * NB)
                load_first_expert(c)
            sp.wait_ge(w_used, 3 * NB * HC)
            sp.dma_start(g_final[:, :], norm_final.rearrange("(a d) -> a d", a=1).partition_broadcast(P)
                         ).then_inc(final_in, 16)

            with sp.Fori(1, NEXP) as e:
                for c in range(NC):
                    if c == 0:
                        sp.wait_ge(no_more_passes, e)
                    if c in (6, 7):
                        sp.wait_ge(first.gu_ps, e)
                    elif c == NC - 1:
                        sp.wait_ge(first.y_ps, e)
                    else:
                        sp.wait_ge(chunk_used, (NC - 3) * (e - 1) + (c // 2 * 2 + 2 if c < 6 else c - 1))
                    sp.dma_start(ring_slot(c), expert_chunk(e, c)).then_inc(chunk_in[c], 16)

            for t in range(NT):
                for j in range(2):
                    sp.wait_ge(out_ready, 2 * t + j + 1)
                    cols = slice(j * D // 2, (j + 1) * D // 2)
                    sp.dma_start(out[0, t * P:(t + 1) * P, cols], acc[:, t, cols]).then_inc(out_stored, 16)
            sp.wait_ge(out_stored, 16 * NT * 2)

        @block.gpsimd
        def _(pool):
            pool.memset(ones[:, :], 1.0).then_inc(p_step, 1)
            pool.memset(eps_col[:, :], EPS).then_inc(consts, 1)
            pool.wait_ge(p_step, 1)
            pool.affine_select(out=ident[:, :], in_=ones[:, :], compare_op=ALU.is_equal, fill=0.0, base=0,
                               pattern=[[-1, P]], channel_multiplier=1).then_inc(consts, 1)
            pool.dma_start(col_rows[0:KD, :], norm_mix.rearrange("a (k p) -> (a k) p", p=P)).then_inc(cols_in, 16)
            pool.dma_start(col_rows[KD:2 * KD, :], norm_ffn.rearrange("a (k p) -> (a k) p", p=P)).then_inc(cols_in, 16)
            pool.dma_start(col_rows[2 * KD:2 * KD + GRP, :], b_s[0]).then_inc(cols_in, 16)
            pool.dma_start(ws_raw, w_s[0].rearrange("g t s -> t g s")).then_inc(ws_in, 16)
            pool.dma_start(w_router[:, :, 0:NGRP], r_w_group[0].rearrange("(k p) n -> p k n", p=P)).then_inc(router_in, 16)
            pool.dma_start(w_router[:, :, NGRP:NR], r_w_exp[0].rearrange("(k p) n -> p k n", p=P)).then_inc(router_in, 16)
            pool.dma_start(b_router[:, 0:NGRP], r_b_group.partition_broadcast(P)).then_inc(router_in, 16)
            pool.dma_start(b_router[:, NGRP:NR], r_b_exp.partition_broadcast(P)).then_inc(router_in, 16)
            pool.dma_start(g_ln, ln_g.partition_broadcast(P)).then_inc(ln_in, 16)
            pool.dma_start(b_ln, ln_b.partition_broadcast(P)).then_inc(ln_in, 16)
            pool.affine_select(out=before[:, :], in_=ones[:, :], compare_op=ALU.is_gt, fill=0.0, base=0,
                               pattern=[[1, P]], channel_multiplier=-1).then_inc(consts, 1)
            pool.iota(iota_cap[:, :], pattern=[[0, NQ], [1, CAP]], base=0, channel_multiplier=0,
                      allow_small_or_imprecise_dtypes=True).then_inc(consts, 1)
            pool.iota(iota_e[:, :], pattern=[[1, NEXP]], base=0, channel_multiplier=0,
                      allow_small_or_imprecise_dtypes=True).then_inc(consts, 1)
            pool.wait_ge(ws_in, 16)
            pool.affine_select(out=ws_raw, in_=ws_raw, compare_op=ALU.is_ge, fill=0.0, base=0,
                               pattern=[[0, GRP], [-1, P]], channel_multiplier=1).then_inc(ws_masked, 1)
            pool.wait_ge(w_used, 3 * NB * HC)
            pool.wait_ge(h_done, NB * NT)
            for t in range(NT):
                pool.tensor_copy(acc[:, t, :], h[:, t, :]).then_inc(acc_init, 1)

        N_CONSTS = 5

        @block.scalar
        def _(act):
            act.wait_ge(x_in[0], 16)
            act.activation(v[:, 0, :], h[:, 0, :], ACT.Square, accum_out=ssq_x[:, 0:1]).then_inc(sumsq_x_done, 1)
            act.wait_ge(cols_ps, 1)
            act.copy(cols_T[:, :], L[:, 0:2 * KD + GRP]).then_inc(cols_done, 1)
            act.wait_ge(cols_done, 1)
            for k in range(KD):
                act.wait_ge(xt_ps, k + 1)
                act.activation(xT_hi[:, k, :], X[k % 2][:, 0:T], ACT.Copy, scale=g_mix[:, k:k + 1]).then_inc(xt_hi, 1)

            def hi_half(n, hc, fresh=False):
                if not fresh:
                    act.wait_ge(w_used, HC * n + hc - 1)
                act.wait_ge(raw_in[hc % 4], 16 * (2 * n + hc // 4 + 1))
                act.copy(w_hi[:, hc % 2, :, :], w_raw[:, hc % 4, :, :]).then_inc(hi_done, 1)

            def gelu_block(n, parity, dst, done):
                act.wait_ge(w_used, HC * (n + 1))
                for t in range(NT):
                    act.activation(dst(t), Z[parity][t][:, :], ACT.Gelu_apprx_tanh,
                                   scale=rstd_x[:, t:t + 1]).then_inc(done, 1)

            for hc in range(HC):
                hi_half(0, hc, fresh=hc < 2)
                if hc == 1:
                    act.activation(v[:, 1, :], h[:, 1, :], ACT.Square, accum_out=ssq_x[:, 1:2]).then_inc(sumsq_x_done, 1)
                    act.wait_ge(sumsq_x_done, 2)
                    act.wait_ge(consts, N_CONSTS)
                    act.activation(rms_x, ssq_x, ACT.Sqrt, scale=1.0 / D, bias=eps_col[:, :]).then_inc(rms_x_done, 1)
            act.wait_ge(rstd_x_done, 1)
            for n in range(1, NB + 1):
                hi_half(n, 0)
                hi_half(n, 1)
                gelu_block(n - 1, (n - 1) % 2, lambda t: v[:, t, (n - 1) * NBLK:n * NBLK], v_ready)
                if n == 2:
                    for i in range(GRP // 2):
                        act.wait_ge(wst_ps, i + 1)
                        act.copy(ws_T[:, 2 * i:2 * i + 2, :], X[i % 2][:, 0:2 * P].rearrange("p (g t) -> p g t", g=2)
                                 ).then_inc(wst_done, 1)
                for hc in range(2, HC):
                    hi_half(n, hc)
            n = NB + 1
            hi_half(n, 0)
            hi_half(n, 1)
            gelu_block(n - 1, 0, lambda t: u[:, 0, t, :], u_ready)
            for hc in range(2, HC):
                hi_half(n, hc)
                if hc == 2:
                    act.wait_ge(var_done, NT)
                    act.activation(std_v, v_mean_var[:, :, 1], ACT.Sqrt, bias=eps_col[:, :]).then_inc(std_done, 1)
            n = NB + 2
            hi_half(n, 0)
            hi_half(n, 1)
            gelu_block(n - 1, 1, lambda t: u[:, 1, t, :], u_ready)
            for g in range(0, GRP, 2):
                for t in range(NT):
                    i = g + t
                    act.wait_ge(sv_ps, i + 1)
                    for j in range(2):
                        r = act.activation(v[:, t, (g + j) * GD:(g + j + 1) * GD], X[i % 2][:, j * GD:(j + 1) * GD],
                                           ACT.Identity, bias=bias_s[:, g + j:g + j + 1])
                    r.then_inc(sv_done, 1)
            for hc in range(2, HC):
                hi_half(n, hc)
            for n in (NB + 3, NB + 4):
                hi_half(n, 0)
                hi_half(n, 1)
                act.wait_ge(y_done, NT * (n - NB - 2))
                gelu_block(n - 1, (n - 1) % 2, lambda t: u[:, (n - 1) % 2, t, :], u_ready)
                if n == NB + 3:
                    for hc in range(2, HC):
                        hi_half(n, hc)
            for i in range(KD // 2):
                act.wait_ge(yt_ps, i + 1)
                act.copy(xT_hi[:, 2 * i:2 * i + 2, :], X[i % 2][:, :].rearrange("p (k t) -> p k t", k=2)
                         ).then_inc(yt_hi, 1)
            for hc in range(2, HC):
                hi_half(2 * NB, hc)

            def sumsq_block(b):
                for t in range(NT):
                    act.wait_ge(h_done, NT * b + t + 1)
                    act.activation(u[:, 1, t, :], h[:, t, b * NBLK:(b + 1) * NBLK], ACT.Square,
                                   accum_out=sumsq_h[:, t, b:b + 1]).then_inc(sumsq_h_done, 1)

            def hgT_block(b):
                for i in range(2):
                    act.wait_ge(ht_ps, 2 * b + i + 1)
                    for j in range(2):
                        k = 4 * b + 2 * i + j
                        r = act.activation(hgT[:, k, :], X[i][:, j * T:(j + 1) * T], ACT.Copy,
                                           scale=g_ffn[:, k:k + 1])
                    r.then_inc(ht_done, 1)

            for b in range(NB - 1):
                n = 2 * NB + 1 + b
                for hc in range(HC):
                    hi_half(n, hc)
                    if hc == 2:
                        sumsq_block(b)
                    if hc == 5:
                        hgT_block(b)
            sumsq_block(NB - 1)
            act.wait_ge(ssq_h_done, 1)
            act.activation(rms_h, ssq_h, ACT.Sqrt, scale=1.0 / D, bias=eps_col[:, :]).then_inc(rms_h_done, 1)
            hgT_block(NB - 1)
            for i in range(2):
                act.wait_ge(exp_in, i + 1)
                src = (rt[:, 1, :, 0:NGRP], rc[:, 4, :])[i]
                act.activation((rt[:, 2, :, 0:NGRP], rc[:, 5, :])[i], src, ACT.Exp).then_inc(exp_done, 1)

            def run_pass(s, n):
                act.wait_ge(s.scat_ps, n + 1)
                act.copy(scatT[:, :, :], Y[:, 0:NT * P].rearrange("p (a t) -> p a t", a=NT)).then_inc(s.scatT, 1)
                act.wait_ge(s.gu_ps, n + 1)
                act.copy(gu[:, :], GU[:, 0:256]).then_inc(s.gu, 1)
                act.wait_ge(s.tr_ps, n + 1)
                act.activation(silu_g[:, :, :], TR[:, 0:256].rearrange("p (b c) -> p b c", b=2)[:, :, 0:2 * CAP],
                               ACT.Silu).then_inc(s.silu, 1)
                act.wait_ge(s.y_ps, n + 1)
                act.copy(y[:, :], Y[:, :]).then_inc(s.y, 1)

            act.wait_ge(counts_ready, 1)
            experts(act, run_pass, after_extra=lambda: act.sem_inc(extras_over, 1))

            for t in range(NT):
                act.wait_ge(first.o_free, NB + NT * NB * (NEXP - 1) + NB * (t + 1))
                act.activation(h[:, t, :], acc[:, t, :], ACT.Square, accum_out=ssq_o[:, t:t + 1]).then_inc(ssq_o_done, 1)
            for t in range(NT):
                act.wait_ge(ssq_o_done, t + 1)
                act.activation(rms_o[:, t:t + 1], ssq_o[:, t:t + 1], ACT.Sqrt, scale=1.0 / D,
                               bias=eps_col[:, :]).then_inc(rms_o_done, 1)

        @block.vector
        def _(dve):
            dve.sem_inc(first.o_free, NB)
            dve.sem_inc(extra.o_free, NB)
            dve.wait_ge(cols_done, 1)
            for k in range(KD):
                dve.wait_ge(xt_hi, k + 1)
                dve.scalar_tensor_tensor(out=xT_lo[:, k, :], in0=X[k % 2][:, 0:T], scalar=g_mix[:, k:k + 1],
                                         in1=xT_hi[:, k, :].bitcast(F32), op0=ALU.mult, op1=ALU.subtract
                                         ).then_inc(xt_lo, 1)

            def lo_half(n, hc):
                dve.wait_ge(hi_done, HC * n + hc + 1)
                dve.tensor_tensor(w_lo[:, hc % 2, :, :], w_raw[:, hc % 4, :, :],
                                  w_hi[:, hc % 2, :, :].bitcast(F32), ALU.subtract).then_inc(lo_done, 1)

            for hc in range(HC):
                lo_half(0, hc)
                if hc == 3:
                    dve.wait_ge(rms_x_done, 1)
                    dve.reciprocal(rstd_x, rms_x).then_inc(rstd_x_done, 1)
            for n in range(1, NB + 1):
                for hc in range(3):
                    lo_half(n, hc)
                for t in range(NT):
                    dve.wait_ge(v_ready, NT * (n - 1) + t + 1)
                    dve.bn_stats(v_stats[:, t, n - 1, :], v[:, t, (n - 1) * NBLK:n * NBLK]).then_inc(ln_step, 1)
                for hc in range(3, HC):
                    lo_half(n, hc)
            n = NB + 1
            lo_half(n, 0)
            dve.wait_ge(ln_step, NT * NB)
            for t in range(NT):
                dve.bn_aggr(v_mean_var[:, t, :], v_stats[:, t, :, :].rearrange("p a b -> p (a b)")).then_inc(var_done, 1)
            lo_half(n, 1)
            lo_half(n, 2)
            dve.wait_ge(std_done, 1)
            dve.wait_ge(ln_in, 32)
            dve.reciprocal(rstd_v, std_v).then_inc(ln_step, 1)
            dve.wait_ge(ln_step, NT * NB + 1)

            def norm_v(t, b):
                cols = slice(b * NBLK, (b + 1) * NBLK)
                dve.scalar_tensor_tensor(out=v[:, t, cols], in0=v[:, t, cols], scalar=v_mean_var[:, t, 0:1],
                                         in1=g_ln[:, cols], op0=ALU.subtract, op1=ALU.mult).then_inc(ln_step, 1)
                dve.wait_ge(ln_step, NT * NB + 2 + NB * t + b)
                dve.scalar_tensor_tensor(out=v[:, t, cols], in0=v[:, t, cols], scalar=rstd_v[:, t:t + 1],
                                         in1=b_ln[:, cols], op0=ALU.mult, op1=ALU.add).then_inc(ln_done, 1)

            norm_v(0, 0)
            for i in range(1, NT * NB):
                if i + 2 < HC:
                    lo_half(n, i + 2)
                norm_v(i // NB, i % NB)

            def gate_v(b):
                for t in range(NT):
                    dve.wait_ge(u_ready, NT * b + t + 1)
                    dve.wait_ge(sv_done, NT * (b + 1))
                    cols = slice(b * NBLK, (b + 1) * NBLK)
                    dve.tensor_tensor(v[:, t, cols], u[:, b % 2, t, :], v[:, t, cols], ALU.mult).then_inc(y_done, 1)

            n = NB + 2
            for hc in range(HC):
                lo_half(n, hc)
                if hc == 1:
                    gate_v(0)
                if hc == 3:
                    gate_v(1)
            n = NB + 3
            for hc in range(HC):
                lo_half(n, hc)
                if hc == 3:
                    gate_v(2)
            lo_half(2 * NB, 0)
            lo_half(2 * NB, 1)
            gate_v(3)
            for i in range(KD // 2):
                dve.wait_ge(yt_hi, i + 1)
                dve.tensor_tensor(xT_lo[:, 2 * i:2 * i + 2, :], X[i % 2][:, :].rearrange("p (k t) -> p k t", k=2),
                                  xT_hi[:, 2 * i:2 * i + 2, :].bitcast(F32), ALU.subtract).then_inc(yt_lo, 1)
            for hc in range(2, HC):
                lo_half(2 * NB, hc)

            def add_x(b):
                dve.wait_ge(w_used, HC * (2 * NB + b + 1))
                for t in range(NT):
                    cols = slice(b * NBLK, (b + 1) * NBLK)
                    dve.tensor_tensor(h[:, t, cols], Z[b % 2][t][:, :], h[:, t, cols], ALU.add).then_inc(h_done, 1)

            for b in range(NB - 1):
                n = 2 * NB + 1 + b
                for hc in range(HC):
                    lo_half(n, hc)
                    if hc == 1:
                        add_x(b)
            add_x(NB - 1)
            dve.wait_ge(sumsq_h_done, NT * NB)
            dve.tensor_reduce(ssq_h, sumsq_h[:, :, :], AX_X, ALU.add).then_inc(ssq_h_done, 1)
            dve.wait_ge(rms_h_done, 1)

            steps = [0]

            def then_step(ins):
                ins.then_inc(r_step, 1)
                steps[0] += 1
                dve.wait_ge(r_step, steps[0])

            def bc(ap, n):
                return ap.unsqueeze(2).to_broadcast([P, NT, n])

            def first_of(onehot, values, best, n, scratch):
                then_step(dve.tensor_tensor(scratch, values, bc(best, n), ALU.is_equal))
                iota = iota_e[:, 0:n].unsqueeze(1).to_broadcast([P, NT, n])
                then_step(dve.tensor_scalar(scratch, scratch, -1000.0, None, ALU.mult))
                then_step(dve.tensor_tensor(scratch, scratch, iota, ALU.add))
                then_step(dve.tensor_reduce(rc[:, 7, :], scratch, AX_X, ALU.min))
                then_step(dve.tensor_tensor(onehot, scratch, bc(rc[:, 7, :], n), ALU.is_equal))

            then_step(dve.reciprocal(rstd_h, rms_h))
            dve.wait_ge(logits_ps, 1)
            dve.wait_ge(router_in, 16 * 4)
            for t in range(NT):
                ins = dve.scalar_tensor_tensor(out=lg[:, t, :], in0=L[:, 64 * t:64 * t + NR],
                                               scalar=rstd_h[:, t:t + 1], in1=b_router[:, :],
                                               op0=ALU.mult, op1=ALU.add)
                ins.then_inc(r_step, 1)
                steps[0] += 1
            dve.wait_ge(r_step, steps[0])
            lg_g, lg_e = lg[:, :, 0:NGRP], lg[:, :, NGRP:NR]
            g_max, g_sum, g_w, m1, d21, e21, w1 = (rc[:, i, :] for i in range(7))
            then_step(dve.tensor_reduce(g_max, lg_g, AX_X, ALU.max))
            dve.tensor_tensor(rt[:, 1, :, 0:NGRP], lg_g, bc(g_max, NGRP), ALU.subtract).then_inc(exp_in, 1)
            group_hot = rt[:, 0, :, 0:NGRP]
            first_of(group_hot, lg_g, g_max, NGRP, rt[:, 3, :, 0:NGRP])
            grp4 = [P, NT, NGRP, EPG]
            hot4 = group_hot.unsqueeze(3).to_broadcast(grp4)
            in_group = rt[:, 4, :, :]
            v4 = in_group.rearrange("p a (g e) -> p a g e", g=NGRP)
            masked, masked2 = rt[:, 5, :, :], rt[:, 6, :, :]
            for t in range(NT):
                ins = dve.tensor_copy(v4[:, t], hot4[:, t])
                ins.then_inc(r_step, 1)
                steps[0] += 1
            dve.wait_ge(r_step, steps[0])
            then_step(dve.tensor_tensor(masked, lg_e, in_group, ALU.mult))
            then_step(dve.tensor_scalar(in_group, in_group, BIG, -BIG, ALU.mult, ALU.add))
            then_step(dve.tensor_tensor(masked, masked, in_group, ALU.add))
            hot1, hot2 = rt[:, 7, :, :], rt[:, 8, :, :]
            then_step(dve.tensor_reduce(m1, masked, AX_X, ALU.max))
            first_of(hot1, masked, m1, NEXP, rt[:, 3, :, :])
            then_step(dve.scalar_tensor_tensor(out=masked2, in0=hot1, scalar=-2 * BIG, in1=masked,
                                               op0=ALU.mult, op1=ALU.add))
            then_step(dve.tensor_reduce(g_w, masked2, AX_X, ALU.max))
            dve.tensor_tensor(d21, g_w, m1, ALU.subtract).then_inc(exp_in, 1)
            first_of(hot2, masked2, g_w, NEXP, rt[:, 3, :, :])
            dve.tensor_tensor(rt[:, 9, :, :], hot1, hot2, ALU.add).then_inc(mask_done, 1)
            dve.wait_ge(exp_done, 2)
            dve.wait_ge(mask_done, 1)
            then_step(dve.tensor_reduce(g_sum, rt[:, 2, :, 0:NGRP], AX_X, ALU.add))
            then_step(dve.reciprocal(g_w, g_sum))
            then_step(dve.tensor_scalar(w1, e21, 1.0, None, ALU.add))
            then_step(dve.reciprocal(w1, w1))
            then_step(dve.tensor_tensor(w1, w1, g_w, ALU.mult))
            then_step(dve.tensor_tensor(g_w, w1, e21, ALU.mult))
            then_step(dve.tensor_tensor(hot1, hot1, bc(w1, NEXP), ALU.mult))
            then_step(dve.tensor_tensor(hot2, hot2, bc(g_w, NEXP), ALU.mult))
            then_step(dve.tensor_tensor(weight_of[:, :, :], hot1, hot2, ALU.add))
            mask = rt[:, 9, :, :]
            off = rt[:, 10, :, :]
            then_step(dve.tensor_scalar(off, mask, -1000.0, 1000.0, ALU.mult, ALU.add))
            dve.wait_ge(ranks_ps, 1)
            then_step(dve.tensor_tensor(rank_of[:, :, :], off, R[:, 0:NT * NEXP].rearrange("p (a e) -> p a e", a=NT),
                                        ALU.add))
            dve.tensor_copy(count_i[:, :], R[:, 128:128 + NEXP]).then_inc(counts_ready, 1)

            def extras():
                n_x, run = rt[:, 0, 0, :], [rt[:, 1, 0, :], rt[:, 2, 0, :]]
                then_step(dve.memset(n_x, 0.0))
                for p in range(1, MAXP):
                    then_step(dve.scalar_tensor_tensor(out=n_x, in0=R[:, 128:128 + NEXP], scalar=float(CAP * p),
                                                       in1=n_x, op0=ALU.is_gt, op1=ALU.add))
                then_step(dve.tensor_copy(extra_i[:, :], n_x))
                then_step(dve.memset(run[0], 0.0))
                then_step(dve.tensor_copy(run[0][:, 1:NEXP], n_x[:, 0:NEXP - 1]))
                shift, a = 1, 0
                while shift < NEXP:
                    then_step(dve.tensor_copy(run[1 - a], run[a]))
                    then_step(dve.tensor_tensor(run[1 - a][:, shift:NEXP], run[a][:, shift:NEXP],
                                                run[a][:, 0:NEXP - shift], ALU.add))
                    shift, a = 2 * shift, 1 - a
                dve.tensor_copy(extra_before_i[:, :], run[a]).then_inc(extra_ready, 1)

            def run_pass(s, n, e_now, iota):
                for t in range(NT):
                    ins = dve.tensor_scalar(sel[:, t, :], iota[:, 0:CAP], rank_of[:, t, bass.ds(e_now, 1)],
                                            rstd_h[:, t:t + 1], ALU.is_equal, ALU.mult)
                ins.then_inc(s.sel, 1)
                for t in range(NT):
                    ins = dve.tensor_scalar(scat[:, t, :], iota[:, :], rank_of[:, t, bass.ds(e_now, 1)],
                                            weight_of[:, t, bass.ds(e_now, 1)], ALU.is_equal, ALU.mult)
                ins.then_inc(s.scat, 1)
                dve.wait_ge(s.gathered, n + 1)
                dve.tensor_tensor(xeT[:, :, :], G[:, :].rearrange("p (k c) -> p k c", c=CAP),
                                  g_ffn.unsqueeze(2).to_broadcast([P, KD, CAP]), ALU.mult).then_inc(s.xe, 1)
                dve.wait_ge(s.silu, n + 1)
                dve.tensor_tensor(hT[:, :, :], silu_g[:, :, :],
                                  TR[:, 0:256].rearrange("p (b c) -> p b c", b=2)[:, :, 2 * CAP:4 * CAP],
                                  ALU.mult).then_inc(s.hT, 1)
                for t in range(NT):
                    for j in range(NB):
                        dve.wait_ge(s.scattered, NT * NB * n + NB * t + j + 1)
                        cols = slice(j * NBLK, (j + 1) * NBLK)
                        dve.tensor_tensor(acc[:, t, cols], O[j][:, :], acc[:, t, cols], ALU.add).then_inc(s.o_free, 1)

            extras()
            dve.wait_ge(acc_init, NT)
            with dve.Fori(0, NEXP) as e:
                count = dve.value_load(count_i[0:1, bass.ds(e, 1)], min_val=0, max_val=T)
                run_pass(first, e, e, iota_cap)
                with dve.If(count > CAP):
                    dve.wait_ge(first.o_free, adds_done(e + 1))
                    n_extra = dve.value_load(extra_i[0:1, bass.ds(e, 1)], min_val=1, max_val=MAXP - 1)
                    n_before = dve.value_load(extra_before_i[0:1, bass.ds(e, 1)], min_val=0, max_val=T * 2 // CAP)
                    dve.tensor_copy(iota_pass[:, :], iota_cap[:, :])
                    with dve.Fori(0, n_extra) as q:
                        dve.drain()
                        dve.tensor_scalar(iota_pass[:, :], iota_pass[:, :], float(CAP), None, ALU.add)
                        dve.drain()
                        run_pass(extra, n_before + q, e, iota_pass)
                    dve.wait_ge(extra.o_free, adds_done(n_before + n_extra))
                    dve.sem_inc(extras_over, 1)
                with dve.Else():
                    dve.nop()

            dve.wait_ge(final_in, 16)
            for t in range(NT):
                dve.wait_ge(rms_o_done, t + 1)
                dve.reciprocal(rstd_o[:, t:t + 1], rms_o[:, t:t + 1]).then_inc(rstd_o_done, 1)
                dve.wait_ge(rstd_o_done, t + 1)
                for j in range(2):
                    cols = slice(j * D // 2, (j + 1) * D // 2)
                    dve.scalar_tensor_tensor(out=acc[:, t, cols], in0=acc[:, t, cols], scalar=rstd_o[:, t:t + 1],
                                             in1=g_final[:, cols], op0=ALU.mult, op1=ALU.mult).then_inc(out_ready, 1)

        @block.tensor
        def _(pe):
            pe.wait_ge(consts, N_CONSTS)
            pe.wait_ge(cols_in, 16 * 3)
            pe.transpose(L[:, 0:2 * KD + GRP], col_rows[:, :], ident[0:2 * KD + GRP, 0:2 * KD + GRP]).then_inc(cols_ps, 1)
            for t in range(NT):
                pe.wait_ge(x_in[t], 16)
            for k in range(KD):
                if k >= 2:
                    pe.wait_ge(xt_lo, k - 1)
                for t in range(NT):
                    ins = pe.transpose(X[k % 2][:, t * P:(t + 1) * P], h[:, t, k * P:(k + 1) * P], ident[:, :])
                ins.then_inc(xt_ps, 1)

            def column_block(n, parity, ready=None, midway=None):
                for hc in range(HC):
                    pe.wait_ge(lo_done, HC * n + hc + 1)
                    for j in range(2):
                        k = 2 * hc + j
                        if ready is not None:
                            ready(k)
                        for t in range(NT):
                            toks = slice(t * P, (t + 1) * P)
                            for part, (a, b) in enumerate(((xT_hi, w_hi), (xT_hi, w_lo), (xT_lo, w_hi))):
                                ins = pe.matmul(Z[parity][t][:, :], a[:, k, toks], b[:, hc % 2, j, :],
                                                start=(k == 0 and part == 0), stop=(k == KD - 1 and part == 2))
                    ins.then_inc(w_used, 1)
                    if hc == HC // 2 - 1 and midway is not None:
                        midway()

            for n in range(NB + 2):
                if 2 <= n < NB + 2:
                    if n - 2 < NB:
                        pe.wait_ge(v_ready, NT * (n - 1))
                column_block(n, n % 2, (lambda k: pe.wait_ge(xt_lo, k + 1)) if n == 0 else None)
                if n == 1:
                    pe.wait_ge(ws_masked, 1)
                    for g in range(0, GRP, 2):
                        i = g // 2
                        if i >= 2:
                            pe.wait_ge(wst_done, i - 1)
                        for j in range(2):
                            ins = pe.transpose(X[i % 2][:, j * P:(j + 1) * P], ws_raw[:, g + j, :], ident[:, :])
                        ins.then_inc(wst_ps, 1)
            pe.wait_ge(wst_done, GRP // 2)
            pe.wait_ge(ln_done, NT * NB)
            for g in range(0, GRP, 2):
                for t in range(NT):
                    i = g + t
                    if i >= 2:
                        pe.wait_ge(sv_done, i - 1)
                    for j in range(2):
                        ins = pe.matmul(X[i % 2][:, j * GD:(j + 1) * GD], ws_T[:, g + j, :],
                                        v[:, t, (g + j) * GD:(g + j + 1) * GD], start=True, stop=True)
                    ins.then_inc(sv_ps, 1)
            for n in (NB + 2, NB + 3):
                pe.wait_ge(u_ready, NT * (n - NB - 1))
                column_block(n, n % 2)
            for i in range(KD // 2):
                pe.wait_ge(y_done, NT * (2 * i // 4 + 1))
                if i >= 2:
                    pe.wait_ge(yt_lo, i - 1)
                for j in range(2):
                    for t in range(NT):
                        ins = pe.transpose(X[i % 2][:, j * T + t * P:j * T + (t + 1) * P],
                                           v[:, t, (2 * i + j) * P:(2 * i + j + 1) * P], ident[:, :])
                ins.then_inc(yt_ps, 1)

            def router_block(b):
                pe.wait_ge(h_done, NT * (b + 1))
                for i in range(2):
                    if b:
                        pe.wait_ge(ht_done, 2 * (b - 1) + i + 1)
                    for j in range(2):
                        k = 4 * b + 2 * i + j
                        for t in range(NT):
                            ins = pe.transpose(X[i][:, j * T + t * P:j * T + (t + 1) * P],
                                               h[:, t, k * P:(k + 1) * P], ident[:, :])
                    ins.then_inc(ht_ps, 1)

            for b in range(NB):
                n = 2 * NB + b
                if b < 2:
                    pe.wait_ge(u_ready, NT * (b + 3))
                else:
                    pe.wait_ge(h_done, NT * (b - 1))
                column_block(n, b % 2, (lambda k: pe.wait_ge(yt_lo, k // 2 + 1)) if b == 0 else None,
                             (lambda: router_block(b - 1)) if b else None)
            router_block(NB - 1)
            pe.wait_ge(router_in, 16 * 4)
            for t in range(NT):
                for k in range(KD):
                    pe.wait_ge(ht_done, k // 2 + 1)
                    ins = pe.matmul(L[:, 64 * t:64 * t + NR], hgT[:, k, t * P:(t + 1) * P], w_router[:, k, :],
                                    start=(k == 0), stop=(k == KD - 1))
            ins.then_inc(logits_ps, 1)
            pe.wait_ge(mask_done, 1)
            mask = rt[:, 9, :, :]
            pe.matmul(R[:, 0:NEXP], before[:, :], mask[:, 0, :], start=True, stop=True)
            pe.matmul(R[:, NEXP:2 * NEXP], ones[:, :], mask[:, 0, :], start=True, stop=False)
            pe.matmul(R[:, NEXP:2 * NEXP], before[:, :], mask[:, 1, :], start=False, stop=True)
            pe.matmul(R[:, 128:128 + NEXP], ones[:, :], mask[:, 0, :], start=True, stop=False)
            pe.matmul(R[:, 128:128 + NEXP], ones[:, :], mask[:, 1, :], start=False, stop=True).then_inc(ranks_ps, 1)

            def run_pass(s, n):
                is_first = s is first
                pe.wait_ge(s.sel, n + 1)
                for k in range(KD):
                    for t in range(NT):
                        ins = pe.matmul(G[:, k * CAP:(k + 1) * CAP], h[:, t, k * P:(k + 1) * P], sel[:, t, :],
                                        start=(t == 0), stop=(t == NT - 1))
                ins.then_inc(s.gathered, 1)
                pe.wait_ge(s.scat, n + 1)
                for t in range(NT):
                    ins = pe.transpose(Y[:, t * P:(t + 1) * P], scat[:, t, :], ident[:, :])
                ins.then_inc(s.scat_ps, 1)
                pe.wait_ge(s.xe, n + 1)
                for kc in range(FT):
                    if is_first:
                        pe.wait_ge(chunk_in[2 * kc], 16 * (n + 1))
                        pe.wait_ge(chunk_in[2 * kc + 1], 16 * (n + 1))
                    for kk in range(KC):
                        k = KC * kc + kk
                        for q in range(NQ):
                            half = kk * FE + (q % 2) * 256
                            ins = pe.matmul(GU[q * CAP:(q + 1) * CAP, 0:256], xeT[:, k, :],
                                            ring[:, 2 * kc + q // 2, half:half + 256],
                                            start=(k == 0), stop=(k == KD - 1))
                    if is_first:
                        if kc < FT - 1:
                            ins.then_inc(chunk_used, 2)
                ins.then_inc(s.gu_ps, 1)
                pe.wait_ge(s.gu, n + 1)
                for b in range(2):
                    ins = pe.transpose(TR[:, b * P:(b + 1) * P], gu[:, b * P:(b + 1) * P], ident[:, :])
                ins.then_inc(s.tr_ps, 1)
                pe.wait_ge(s.hT, n + 1)
                pe.wait_ge(s.scatT, n + 1)
                for f in range(FT):
                    if is_first:
                        pe.wait_ge(chunk_in[8 + f], 16 * (n + 1))
                    for j in range(NB):
                        ins = pe.matmul(Y[j * CAP:(j + 1) * CAP, :], hT[:, f % 2, (f // 2) * CAP:(f // 2 + 1) * CAP],
                                        ring[:, 8 + f, j * NBLK:(j + 1) * NBLK], start=(f == 0), stop=(f == FT - 1))
                    if is_first and f < FT - 1:
                        ins.then_inc(chunk_used, 1)
                ins.then_inc(s.y_ps, 1)
                pe.wait_ge(s.y, n + 1)
                for t in range(NT):
                    for j in range(NB):
                        pe.wait_ge(s.o_free, NT * NB * n + NB * t + j + 1)
                        pe.matmul(O[j][:, :], scatT[j * CAP:(j + 1) * CAP, t, :], y[j * CAP:(j + 1) * CAP, :],
                                  start=True, stop=True).then_inc(s.scattered, 1)

            pe.wait_ge(counts_ready, 1)
            experts(pe, run_pass, at_start=lambda: pe.sem_inc(no_more_passes, 1),
                    after_extra=lambda: pe.sem_inc(no_more_passes, 1))


_INS = ["x", "norm_mix", "norm_ffn", "norm_final", "a_w_in", "a_ln_g", "a_ln_b", "a_w_s", "a_b_s", "a_w_out",
        "r_w_group", "r_b_group", "r_w_exp", "r_b_exp", "e_w_gate", "e_w_up", "e_w_down"]


def kernel(**inputs):
    import numpy as _np
    import concourse.bacc as _bacc
    from concourse.bass_utils import run_bass_kernel_spmd as _run

    nc = _bacc.Bacc("TRN2", target_bir_lowering=False, num_devices=1)
    arrays, args = {}, []
    for name in _INS:
        a = _np.ascontiguousarray(inputs[name])
        arrays[f"in_{name}"] = a
        args.append(nc.dram_tensor(f"in_{name}", a.shape, mybir.dt.from_np(a.dtype), kind="ExternalInput").ap())
    out = nc.dram_tensor("out_h", inputs["x"].shape, F32, kind="ExternalOutput").ap()
    hybrid_layer(nc, *args, out)
    r = _run(nc, [arrays], core_ids=[0])
    return r.results[0]["out_h"]
```

```python
from contextlib import ExitStack

import concourse.bass as bass
from concourse import mybir

F32 = mybir.dt.float32
F32R = mybir.dt.float32r
I32 = mybir.dt.int32
ALU = mybir.AluOpType
ACT = mybir.ActivationFunctionType
AX_X = mybir.AxisListType.X

P = 128
EPS = 1e-6
CAP = 32
BIG = 1.0e30


def hybrid_layer(nc, x, norm_mix, norm_ffn, norm_final, w_in, ln_g, ln_b, w_s, b_s, w_out,
                 r_w_group, r_b_group, r_w_exp, r_b_exp, e_gate, e_up, e_down, out):
    _, T, D = x.shape
    NT = T // P
    KD = D // P
    NBLK = 512
    NB = D // NBLK
    GRP = w_s.shape[1]
    GD = D // GRP
    NGRP = r_w_group.shape[2]
    NEXP = r_w_exp.shape[2]
    EPG = NEXP // NGRP
    NR = NGRP + NEXP
    FE = e_gate.shape[3]
    FT = FE // P
    NC = 12
    KC = 4
    HC = 8
    NQ = P // CAP
    MAXP = T // CAP
    assert (NT, KD, NB, FT, NQ, GD, NGRP * EPG) == (2, 16, 4, 4, 4, 256, NEXP)

    with ExitStack() as ctx:
        def sem(name):
            return ctx.enter_context(nc.semaphore(name))

        def sb(name, shape, dt=F32, stack=ctx):
            return stack.enter_context(nc.sbuf_tensor(name, shape, dt))

        ring = sb("ring", [P, NC, 2048])
        h = sb("h", [P, NT, D])
        v = sb("v", [P, NT, D])
        ident = sb("ident", [P, P])
        iota_cap = sb("iota_cap", [P, CAP])
        before = sb("before", [P, P])
        ones = sb("ones", [P, P])
        w_router = sb("w_router", [P, KD, NR])
        b_router = sb("b_router", [P, NR])
        col_rows = sb("col_rows", [2 * KD + GRP, P])
        cols_T = sb("cols_T", [P, 2 * KD + GRP])
        g_mix, g_ffn, bias_s = cols_T[:, 0:KD], cols_T[:, KD:2 * KD], cols_T[:, 2 * KD:2 * KD + GRP]
        v_stats = sb("v_stats", [P, NT, NB, 6])
        v_mean_var = sb("v_mean_var", [P, NT, 2])
        rows = sb("rows", [P, 12, NT])
        sumsq_h = sb("sumsq_h", [P, NT, NB])
        eps_col = sb("eps_col", [P, 1])
        iota_e = sb("iota_e", [P, NEXP])
        rank_of = sb("rank_of", [P, NT, NEXP])
        weight_of = sb("weight_of", [P, NT, NEXP])
        count_i = sb("count_i", [P, NEXP], I32)
        extra_i = sb("extra_i", [P, NEXP], I32)
        extra_before_i = sb("extra_before_i", [P, NEXP], I32)
        rstd_x, rms_x, ssq_x, rstd_v, std_v = (rows[:, i, :] for i in range(5))
        rstd_h, rms_h, ssq_h, rstd_o, rms_o, ssq_o = (rows[:, i, :] for i in range(5, 11))

        with ExitStack() as mixer:
            xT_hi = sb("xT_hi", [P, KD, T], F32R, mixer)
            xT_lo = sb("xT_lo", [P, KD, T], F32R, mixer)
            w_raw = sb("w_raw", [P, 4, 2, NBLK], F32, mixer)
            w_hi = sb("w_hi", [P, 2, 2, NBLK], F32R, mixer)
            w_lo = sb("w_lo", [P, 2, 2, NBLK], F32R, mixer)
            u = sb("u", [P, 2, NT, NBLK], F32, mixer)
        acc = sb("acc", [P, NT, D])
        g_final = sb("g_final", [P, D])
        xe = sb("xe", [P, NBLK])
        xeT = sb("xeT", [P, KC, NQ, CAP])
        gu = sb("gu", [P, 256])
        silu_g = sb("silu_g", [P, 2, 2 * CAP])
        hT = sb("hT", [P, 2, 2 * CAP])
        y = sb("y", [P, D])
        scatT = sb("scatT", [P, NT, P])
        y_x = sb("y_x", [CAP, D])
        scatT_x = sb("scatT_x", [CAP, NT, P])
        scat = sb("scat", [P, NT, P])
        scat_x = sb("scat_x", [P, NT, CAP])
        sel = sb("sel", [P, NT, CAP])
        iota_pass = sb("iota_pass", [P, CAP])
        lg = sb("lg", [P, NT, NR])
        rt = sb("rt", [P, 12, NT, NEXP])
        rc = sb("rc", [P, 8, NT])

        ws_raw = ring[:, 9, 0:GRP * P].rearrange("p (g s) -> p g s", g=GRP)
        ws_T = ring[:, 9, GRP * P:2 * GRP * P].rearrange("p (g s) -> p g s", g=GRP)
        g_ln, b_ln = ring[:, 10, :], ring[:, 11, :]
        hgT = v[:, :, :].rearrange("p a (b t) -> p (a b) t", t=T)

        bank = [ctx.enter_context(nc.psum_tensor(f"bank{i}", [P, NBLK], F32)) for i in range(8)]
        Z = [[bank[0], bank[1]], [bank[2], bank[3]]]
        X = [bank[4], bank[5]]
        L = bank[6]
        R = bank[7]
        O = [bank[0], bank[1], bank[2], bank[3]]
        XE, GU, TR, Y = bank[4], bank[5], bank[6], bank[7]

        x_in = [sem(f"x_in{t}") for t in range(NT)]
        raw_in = [sem(f"raw_in{s}") for s in range(4)]
        chunk_in = [sem(f"chunk_in{c}") for c in range(NC)]
        cols_in, cols_ps, cols_done = sem("cols_in"), sem("cols_ps"), sem("cols_done")
        ws_in, router_in, ln_in, final_in = sem("ws_in"), sem("router_in"), sem("ln_in"), sem("final_in")
        consts, ws_masked = sem("consts"), sem("ws_masked")
        xt_ps, xt_hi, xt_lo = sem("xt_ps"), sem("xt_hi"), sem("xt_lo")
        hi_done, lo_done, w_used = sem("hi_done"), sem("lo_done"), sem("w_used")
        v_ready, u_ready, y_done = sem("v_ready"), sem("u_ready"), sem("y_done")
        ln_step, ln_done, var_done, std_done = sem("ln_step"), sem("ln_done"), sem("var_done"), sem("std_done")
        wst_ps, wst_done = sem("wst_ps"), sem("wst_done")
        sv_ps, sv_done = sem("sv_ps"), sem("sv_done")
        yt_ps, yt_hi, yt_lo = sem("yt_ps"), sem("yt_hi"), sem("yt_lo")
        sumsq_x_done, rms_x_done, rstd_x_done = sem("sumsq_x_done"), sem("rms_x_done"), sem("rstd_x_done")
        h_done, sumsq_h_done = sem("h_done"), sem("sumsq_h_done")
        ht_ps, ht_done = sem("ht_ps"), sem("ht_done")
        ssq_h_done, rms_h_done = sem("ssq_h_done"), sem("rms_h_done")
        logits_ps, mask_done, ranks_ps, exp_in, exp_done = (
            sem("logits_ps"), sem("mask_done"), sem("ranks_ps"), sem("exp_in"), sem("exp_done"))
        r_step, counts_ready, extra_ready, p_step = (
            sem("r_step"), sem("counts_ready"), sem("extra_ready"), sem("p_step"))
        acc_init, iota_moved = sem("acc_init"), sem("iota_moved")
        extras_over = sem("extras_over")
        chunk_used, no_more_passes = sem("chunk_used"), sem("no_more_passes")
        ssq_o_done, rms_o_done, rstd_o_done, out_ready, out_stored = (
            sem("ssq_o_done"), sem("rms_o_done"), sem("rstd_o_done"), sem("out_ready"), sem("out_stored"))

        class PassSems:

            def __init__(self, s):
                self.sel = sem(f"sel_ready{s}")
                self.xe_ps = sem(f"xe_ps{s}")
                self.xe = sem(f"xe_ready{s}")
                self.xeT_ps = sem(f"xeT_ps{s}")
                self.xeT = sem(f"xeT_ready{s}")
                self.gu_ps = sem(f"gu_ps{s}")
                self.gu = sem(f"gu_ready{s}")
                self.tr_ps = sem(f"tr_ps{s}")
                self.silu = sem(f"silu_ready{s}")
                self.hT = sem(f"hT_ready{s}")
                self.y_ps = sem(f"y_ps{s}")
                self.y = sem(f"y_ready{s}")
                self.scat_ps = sem(f"scat_ps{s}")
                self.scatT = sem(f"scatT_ready{s}")
                self.scattered = sem(f"scattered{s}")
                self.o_free = sem(f"o_free{s}")

        first, extra = PassSems(""), PassSems("_x")

        def adds_done(n_scatters):
            return n_scatters * NT * NB + NB

        def w_in_half(col, hc):
            return w_in[0, hc * 2 * P:(hc + 1) * 2 * P, bass.ds(col, NBLK)].rearrange("(j p) n -> p j n", p=P)

        def w_out_half(col, hc):
            return w_out[0, hc * 2 * P:(hc + 1) * 2 * P, col:col + NBLK].rearrange("(j p) n -> p j n", p=P)

        def expert_chunk(e, c):
            if c < 8:
                w, k = (e_gate, e_up)[c % 2], c // 2
                return w[0, e, k * KC * P:(k + 1) * KC * P, :].rearrange("(j p) n -> p j n", p=P)
            return e_down[0, e, (c - 8) * P:(c - 7) * P, :]

        def ring_slot(c):
            return ring[:, c, :].rearrange("p (j n) -> p j n", j=KC) if c < 8 else ring[:, c, :]

        def experts(eng, run_pass, scatter, after_extra, at_start=None, before_extra=None):
            with eng.Fori(0, NEXP // NQ) as g:
                for q in range(NQ):
                    e = NQ * g + q
                    count = eng.value_load(count_i[0:1, bass.ds(e, 1)], min_val=0, max_val=T)
                    if at_start is not None:
                        with eng.If(count <= CAP):
                            at_start()
                        with eng.Else():
                            eng.nop()
                    run_pass(first, e, q, e, g)
                    with eng.If(count > CAP):
                        eng.wait_ge(extra_ready, 1)
                        eng.wait_ge(first.y, e + 1)
                        eng.wait_ge(first.o_free, NT * NB * g + NB)
                        n_extra = eng.value_load(extra_i[0:1, bass.ds(e, 1)], min_val=1, max_val=MAXP - 1)
                        n_before = eng.value_load(extra_before_i[0:1, bass.ds(e, 1)], min_val=0,
                                                  max_val=T * 2 // CAP)
                        if before_extra is not None:
                            before_extra()
                        with eng.Fori(0, n_extra) as i:
                            run_pass(extra, n_before + i, 0, e, None)
                            scatter(extra, n_before + i)
                        eng.wait_ge(extra.o_free, adds_done(n_before + n_extra))
                        after_extra()
                    with eng.Else():
                        eng.nop()
                scatter(first, g)

        block = ctx.enter_context(nc.Block())

        @block.sync
        def _(sp):
            for t in range(NT):
                sp.dma_start(h[:, t, :], x[0, t * P:(t + 1) * P, :]).then_inc(x_in[t], 16)

            def load_half(src, n, hc, first_block=False):
                if not (first_block and hc < 4):
                    sp.wait_ge(lo_done, HC * n + hc - 3)
                sp.dma_start(w_raw[:, hc % 4, :, :], src).then_inc(raw_in[hc % 4], 16)

            def load_first_expert(c):
                sp.dma_start(ring_slot(c), expert_chunk(0, c)).then_inc(chunk_in[c], 16)

            for n in range(2 * NB):
                col = D + n * NBLK if n < NB else (n - NB) * NBLK
                for hc in range(HC):
                    load_half(w_in_half(col, hc), n, hc, n == 0)
                load_first_expert(n)
            for n in range(NB):
                for hc in range(HC):
                    load_half(w_out_half(n * NBLK, hc), 2 * NB + n, hc)
                c = 2 * NB + n
                if c == 9:
                    sp.wait_ge(sv_ps, NT * GRP // 2)
                if c == 10:
                    sp.wait_ge(ln_done, NT * NB)
                load_first_expert(c)
            sp.wait_ge(w_used, 3 * NB * HC)
            sp.dma_start(g_final[:, :], norm_final.rearrange("(a d) -> a d", a=1).partition_broadcast(P)
                         ).then_inc(final_in, 16)

            with sp.Fori(1, NEXP) as e:
                for c in range(NC):
                    if c == 0:
                        sp.wait_ge(no_more_passes, e)
                    if c in (6, 7):
                        sp.wait_ge(first.gu_ps, e)
                    elif c == NC - 1:
                        sp.wait_ge(first.y_ps, e)
                    else:
                        sp.wait_ge(chunk_used, (NC - 3) * (e - 1) + (c // 2 * 2 + 2 if c < 6 else c - 1))
                    sp.dma_start(ring_slot(c), expert_chunk(e, c)).then_inc(chunk_in[c], 16)

            for t in range(NT):
                for j in range(2):
                    sp.wait_ge(out_ready, 2 * t + j + 1)
                    cols = slice(j * D // 2, (j + 1) * D // 2)
                    sp.dma_start(out[0, t * P:(t + 1) * P, cols], acc[:, t, cols]).then_inc(out_stored, 16)
            sp.wait_ge(out_stored, 16 * NT * 2)

        @block.gpsimd
        def _(pool):
            pool.memset(ones[:, :], 1.0).then_inc(p_step, 1)
            pool.memset(eps_col[:, :], EPS).then_inc(consts, 1)
            pool.wait_ge(p_step, 1)
            pool.affine_select(out=ident[:, :], in_=ones[:, :], compare_op=ALU.is_equal, fill=0.0, base=0,
                               pattern=[[-1, P]], channel_multiplier=1).then_inc(consts, 1)
            pool.dma_start(col_rows[0:KD, :], norm_mix.rearrange("a (k p) -> (a k) p", p=P)).then_inc(cols_in, 16)
            pool.dma_start(col_rows[KD:2 * KD, :], norm_ffn.rearrange("a (k p) -> (a k) p", p=P)).then_inc(cols_in, 16)
            pool.dma_start(col_rows[2 * KD:2 * KD + GRP, :], b_s[0]).then_inc(cols_in, 16)
            pool.dma_start(ws_raw, w_s[0].rearrange("g t s -> t g s")).then_inc(ws_in, 16)
            pool.dma_start(w_router[:, :, 0:NGRP], r_w_group[0].rearrange("(k p) n -> p k n", p=P)).then_inc(router_in, 16)
            pool.dma_start(w_router[:, :, NGRP:NR], r_w_exp[0].rearrange("(k p) n -> p k n", p=P)).then_inc(router_in, 16)
            pool.dma_start(b_router[:, 0:NGRP], r_b_group.partition_broadcast(P)).then_inc(router_in, 16)
            pool.dma_start(b_router[:, NGRP:NR], r_b_exp.partition_broadcast(P)).then_inc(router_in, 16)
            pool.dma_start(g_ln, ln_g.partition_broadcast(P)).then_inc(ln_in, 16)
            pool.dma_start(b_ln, ln_b.partition_broadcast(P)).then_inc(ln_in, 16)
            pool.affine_select(out=before[:, :], in_=ones[:, :], compare_op=ALU.is_gt, fill=0.0, base=0,
                               pattern=[[1, P]], channel_multiplier=-1).then_inc(consts, 1)
            pool.iota(iota_cap[:, :], pattern=[[1, CAP]], base=0, channel_multiplier=0,
                      allow_small_or_imprecise_dtypes=True).then_inc(consts, 1)
            pool.iota(iota_e[:, :], pattern=[[1, NEXP]], base=0, channel_multiplier=0,
                      allow_small_or_imprecise_dtypes=True).then_inc(consts, 1)
            pool.wait_ge(ws_in, 16)
            pool.affine_select(out=ws_raw, in_=ws_raw, compare_op=ALU.is_ge, fill=0.0, base=0,
                               pattern=[[0, GRP], [-1, P]], channel_multiplier=1).then_inc(ws_masked, 1)
            pool.wait_ge(w_used, 3 * NB * HC)
            pool.wait_ge(h_done, NB * NT)
            for t in range(NT):
                pool.tensor_copy(acc[:, t, :], h[:, t, :]).then_inc(acc_init, 1)

        N_CONSTS = 5

        @block.scalar
        def _(act):
            act.wait_ge(x_in[0], 16)
            act.activation(v[:, 0, :], h[:, 0, :], ACT.Square, accum_out=ssq_x[:, 0:1]).then_inc(sumsq_x_done, 1)
            act.wait_ge(cols_ps, 1)
            act.copy(cols_T[:, :], L[:, 0:2 * KD + GRP]).then_inc(cols_done, 1)
            act.wait_ge(cols_done, 1)
            for k in range(KD):
                act.wait_ge(xt_ps, k + 1)
                act.activation(xT_hi[:, k, :], X[k % 2][:, 0:T], ACT.Copy, scale=g_mix[:, k:k + 1]).then_inc(xt_hi, 1)

            def hi_half(n, hc, fresh=False):
                if not fresh:
                    act.wait_ge(w_used, HC * n + hc - 1)
                act.wait_ge(raw_in[hc % 4], 16 * (2 * n + hc // 4 + 1))
                act.copy(w_hi[:, hc % 2, :, :], w_raw[:, hc % 4, :, :]).then_inc(hi_done, 1)

            def gelu_block(n, parity, dst, done):
                act.wait_ge(w_used, HC * (n + 1))
                for t in range(NT):
                    act.activation(dst(t), Z[parity][t][:, :], ACT.Gelu_apprx_tanh,
                                   scale=rstd_x[:, t:t + 1]).then_inc(done, 1)

            for hc in range(HC):
                hi_half(0, hc, fresh=hc < 2)
                if hc == 1:
                    act.activation(v[:, 1, :], h[:, 1, :], ACT.Square, accum_out=ssq_x[:, 1:2]).then_inc(sumsq_x_done, 1)
                    act.wait_ge(sumsq_x_done, 2)
                    act.wait_ge(consts, N_CONSTS)
                    act.activation(rms_x, ssq_x, ACT.Sqrt, scale=1.0 / D, bias=eps_col[:, :]).then_inc(rms_x_done, 1)
            act.wait_ge(rstd_x_done, 1)
            for n in range(1, NB + 1):
                hi_half(n, 0)
                hi_half(n, 1)
                gelu_block(n - 1, (n - 1) % 2, lambda t: v[:, t, (n - 1) * NBLK:n * NBLK], v_ready)
                if n == 2:
                    for i in range(GRP // 2):
                        act.wait_ge(wst_ps, i + 1)
                        act.copy(ws_T[:, 2 * i:2 * i + 2, :], X[i % 2][:, 0:2 * P].rearrange("p (g t) -> p g t", g=2)
                                 ).then_inc(wst_done, 1)
                for hc in range(2, HC):
                    hi_half(n, hc)
            n = NB + 1
            hi_half(n, 0)
            hi_half(n, 1)
            gelu_block(n - 1, 0, lambda t: u[:, 0, t, :], u_ready)
            for hc in range(2, HC):
                hi_half(n, hc)
                if hc == 2:
                    act.wait_ge(var_done, NT)
                    act.activation(std_v, v_mean_var[:, :, 1], ACT.Sqrt, bias=eps_col[:, :]).then_inc(std_done, 1)
            n = NB + 2
            hi_half(n, 0)
            hi_half(n, 1)
            gelu_block(n - 1, 1, lambda t: u[:, 1, t, :], u_ready)
            for g in range(0, GRP, 2):
                for t in range(NT):
                    i = g + t
                    act.wait_ge(sv_ps, i + 1)
                    for j in range(2):
                        r = act.activation(v[:, t, (g + j) * GD:(g + j + 1) * GD], X[i % 2][:, j * GD:(j + 1) * GD],
                                           ACT.Identity, bias=bias_s[:, g + j:g + j + 1])
                    r.then_inc(sv_done, 1)
            for hc in range(2, HC):
                hi_half(n, hc)
            for n in (NB + 3, NB + 4):
                hi_half(n, 0)
                hi_half(n, 1)
                act.wait_ge(y_done, NT * (n - NB - 2))
                gelu_block(n - 1, (n - 1) % 2, lambda t: u[:, (n - 1) % 2, t, :], u_ready)
                if n == NB + 3:
                    for hc in range(2, HC):
                        hi_half(n, hc)
            for i in range(KD // 2):
                act.wait_ge(yt_ps, i + 1)
                act.copy(xT_hi[:, 2 * i:2 * i + 2, :], X[i % 2][:, :].rearrange("p (k t) -> p k t", k=2)
                         ).then_inc(yt_hi, 1)
            for hc in range(2, HC):
                hi_half(2 * NB, hc)

            def sumsq_block(b):
                for t in range(NT):
                    act.wait_ge(h_done, NT * b + t + 1)
                    act.activation(u[:, 1, t, :], h[:, t, b * NBLK:(b + 1) * NBLK], ACT.Square,
                                   accum_out=sumsq_h[:, t, b:b + 1]).then_inc(sumsq_h_done, 1)

            def hgT_block(b):
                for i in range(2):
                    act.wait_ge(ht_ps, 2 * b + i + 1)
                    for j in range(2):
                        k = 4 * b + 2 * i + j
                        r = act.activation(hgT[:, k, :], X[i][:, j * T:(j + 1) * T], ACT.Copy,
                                           scale=g_ffn[:, k:k + 1])
                    r.then_inc(ht_done, 1)

            for b in range(NB - 1):
                n = 2 * NB + 1 + b
                for hc in range(HC):
                    hi_half(n, hc)
                    if hc == 2:
                        sumsq_block(b)
                    if hc == 5:
                        hgT_block(b)
            sumsq_block(NB - 1)
            act.wait_ge(ssq_h_done, 1)
            act.activation(rms_h, ssq_h, ACT.Sqrt, scale=1.0 / D, bias=eps_col[:, :]).then_inc(rms_h_done, 1)
            hgT_block(NB - 1)
            for i in range(2):
                act.wait_ge(exp_in, i + 1)
                src = (rt[:, 1, :, 0:NGRP], rc[:, 4, :])[i]
                act.activation((rt[:, 2, :, 0:NGRP], rc[:, 5, :])[i], src, ACT.Exp).then_inc(exp_done, 1)

            def run_pass(s, n, q, e, g):
                act.activation(rows[:, 11, 0:1], eps_col[:, :], ACT.Silu)
                act.wait_ge(s.xe_ps, n + 1)
                act.copy(xe[:, :], XE[:, :]).then_inc(s.xe, 1)
                act.wait_ge(s.gu_ps, n + 1)
                act.copy(gu[:, :], GU[:, 0:256]).then_inc(s.gu, 1)
                act.wait_ge(s.tr_ps, n + 1)
                act.activation(silu_g[:, :, :], TR[:, 0:256].rearrange("p (b c) -> p b c", b=2)[:, :, 0:2 * CAP],
                               ACT.Silu).then_inc(s.silu, 1)
                act.wait_ge(s.y_ps, n + 1)
                dst = y[q * CAP:(q + 1) * CAP, :] if s is first else y_x[:, :]
                for j in range(NB):
                    ins = act.copy(dst[:, j * NBLK:(j + 1) * NBLK], Y[j * CAP:(j + 1) * CAP, :])
                ins.then_inc(s.y, 1)

            def scatter(s, m):
                act.wait_ge(s.scat_ps, m + 1)
                if s is first:
                    act.copy(scatT[:, :, :], XE[:, 0:NT * P].rearrange("p (a t) -> p a t", a=NT)).then_inc(s.scatT, 1)
                else:
                    act.copy(scatT_x[:, :, :], XE[0:CAP, 0:NT * P].rearrange("p (a t) -> p a t", a=NT)
                             ).then_inc(s.scatT, 1)

            act.wait_ge(counts_ready, 1)
            experts(act, run_pass, scatter, after_extra=lambda: act.sem_inc(extras_over, 1))

            for t in range(NT):
                act.wait_ge(first.o_free, adds_done(NEXP // NQ - 1) + NB * (t + 1))
                act.activation(h[:, t, :], acc[:, t, :], ACT.Square, accum_out=ssq_o[:, t:t + 1]).then_inc(ssq_o_done, 1)
            for t in range(NT):
                act.wait_ge(ssq_o_done, t + 1)
                act.activation(rms_o[:, t:t + 1], ssq_o[:, t:t + 1], ACT.Sqrt, scale=1.0 / D,
                               bias=eps_col[:, :]).then_inc(rms_o_done, 1)

        @block.vector
        def _(dve):
            dve.sem_inc(first.o_free, NB)
            dve.sem_inc(extra.o_free, NB)
            dve.wait_ge(cols_done, 1)
            for k in range(KD):
                dve.wait_ge(xt_hi, k + 1)
                dve.scalar_tensor_tensor(out=xT_lo[:, k, :], in0=X[k % 2][:, 0:T], scalar=g_mix[:, k:k + 1],
                                         in1=xT_hi[:, k, :].bitcast(F32), op0=ALU.mult, op1=ALU.subtract
                                         ).then_inc(xt_lo, 1)

            def lo_half(n, hc):
                dve.wait_ge(hi_done, HC * n + hc + 1)
                dve.tensor_tensor(w_lo[:, hc % 2, :, :], w_raw[:, hc % 4, :, :],
                                  w_hi[:, hc % 2, :, :].bitcast(F32), ALU.subtract).then_inc(lo_done, 1)

            for hc in range(HC):
                lo_half(0, hc)
                if hc == 3:
                    dve.wait_ge(rms_x_done, 1)
                    dve.reciprocal(rstd_x, rms_x).then_inc(rstd_x_done, 1)
            for n in range(1, NB + 1):
                for hc in range(3):
                    lo_half(n, hc)
                for t in range(NT):
                    dve.wait_ge(v_ready, NT * (n - 1) + t + 1)
                    dve.bn_stats(v_stats[:, t, n - 1, :], v[:, t, (n - 1) * NBLK:n * NBLK]).then_inc(ln_step, 1)
                for hc in range(3, HC):
                    lo_half(n, hc)
            n = NB + 1
            lo_half(n, 0)
            dve.wait_ge(ln_step, NT * NB)
            for t in range(NT):
                dve.bn_aggr(v_mean_var[:, t, :], v_stats[:, t, :, :].rearrange("p a b -> p (a b)")).then_inc(var_done, 1)
            lo_half(n, 1)
            lo_half(n, 2)
            dve.wait_ge(std_done, 1)
            dve.wait_ge(ln_in, 32)
            dve.reciprocal(rstd_v, std_v).then_inc(ln_step, 1)
            dve.wait_ge(ln_step, NT * NB + 1)

            def norm_v(t, b):
                cols = slice(b * NBLK, (b + 1) * NBLK)
                dve.scalar_tensor_tensor(out=v[:, t, cols], in0=v[:, t, cols], scalar=v_mean_var[:, t, 0:1],
                                         in1=g_ln[:, cols], op0=ALU.subtract, op1=ALU.mult).then_inc(ln_step, 1)
                dve.wait_ge(ln_step, NT * NB + 2 + NB * t + b)
                dve.scalar_tensor_tensor(out=v[:, t, cols], in0=v[:, t, cols], scalar=rstd_v[:, t:t + 1],
                                         in1=b_ln[:, cols], op0=ALU.mult, op1=ALU.add).then_inc(ln_done, 1)

            norm_v(0, 0)
            for i in range(1, NT * NB):
                if i + 2 < HC:
                    lo_half(n, i + 2)
                norm_v(i // NB, i % NB)

            def gate_v(b):
                for t in range(NT):
                    dve.wait_ge(u_ready, NT * b + t + 1)
                    dve.wait_ge(sv_done, NT * (b + 1))
                    cols = slice(b * NBLK, (b + 1) * NBLK)
                    dve.tensor_tensor(v[:, t, cols], u[:, b % 2, t, :], v[:, t, cols], ALU.mult).then_inc(y_done, 1)

            n = NB + 2
            for hc in range(HC):
                lo_half(n, hc)
                if hc == 1:
                    gate_v(0)
                if hc == 3:
                    gate_v(1)
            n = NB + 3
            for hc in range(HC):
                lo_half(n, hc)
                if hc == 3:
                    gate_v(2)
            lo_half(2 * NB, 0)
            lo_half(2 * NB, 1)
            gate_v(3)
            for i in range(KD // 2):
                dve.wait_ge(yt_hi, i + 1)
                dve.tensor_tensor(xT_lo[:, 2 * i:2 * i + 2, :], X[i % 2][:, :].rearrange("p (k t) -> p k t", k=2),
                                  xT_hi[:, 2 * i:2 * i + 2, :].bitcast(F32), ALU.subtract).then_inc(yt_lo, 1)
            for hc in range(2, HC):
                lo_half(2 * NB, hc)

            def add_x(b):
                dve.wait_ge(w_used, HC * (2 * NB + b + 1))
                for t in range(NT):
                    cols = slice(b * NBLK, (b + 1) * NBLK)
                    dve.tensor_tensor(h[:, t, cols], Z[b % 2][t][:, :], h[:, t, cols], ALU.add).then_inc(h_done, 1)

            for b in range(NB - 1):
                n = 2 * NB + 1 + b
                for hc in range(HC):
                    lo_half(n, hc)
                    if hc == 1:
                        add_x(b)
            add_x(NB - 1)
            dve.wait_ge(sumsq_h_done, NT * NB)
            dve.tensor_reduce(ssq_h, sumsq_h[:, :, :], AX_X, ALU.add).then_inc(ssq_h_done, 1)
            dve.wait_ge(rms_h_done, 1)

            steps = [0]

            def then_step(ins):
                ins.then_inc(r_step, 1)
                steps[0] += 1
                dve.wait_ge(r_step, steps[0])

            def bc(ap, n):
                return ap.unsqueeze(2).to_broadcast([P, NT, n])

            def first_of(onehot, values, best, n, scratch):
                then_step(dve.tensor_tensor(scratch, values, bc(best, n), ALU.is_equal))
                iota = iota_e[:, 0:n].unsqueeze(1).to_broadcast([P, NT, n])
                then_step(dve.tensor_scalar(scratch, scratch, -1000.0, None, ALU.mult))
                then_step(dve.tensor_tensor(scratch, scratch, iota, ALU.add))
                then_step(dve.tensor_reduce(rc[:, 7, :], scratch, AX_X, ALU.min))
                then_step(dve.tensor_tensor(onehot, scratch, bc(rc[:, 7, :], n), ALU.is_equal))

            then_step(dve.reciprocal(rstd_h, rms_h))
            dve.wait_ge(logits_ps, 1)
            dve.wait_ge(router_in, 16 * 4)
            for t in range(NT):
                ins = dve.scalar_tensor_tensor(out=lg[:, t, :], in0=L[:, 64 * t:64 * t + NR],
                                               scalar=rstd_h[:, t:t + 1], in1=b_router[:, :],
                                               op0=ALU.mult, op1=ALU.add)
                ins.then_inc(r_step, 1)
                steps[0] += 1
            dve.wait_ge(r_step, steps[0])
            lg_g, lg_e = lg[:, :, 0:NGRP], lg[:, :, NGRP:NR]
            g_max, g_sum, g_w, m1, d21, e21, w1 = (rc[:, i, :] for i in range(7))
            then_step(dve.tensor_reduce(g_max, lg_g, AX_X, ALU.max))
            dve.tensor_tensor(rt[:, 1, :, 0:NGRP], lg_g, bc(g_max, NGRP), ALU.subtract).then_inc(exp_in, 1)
            group_hot = rt[:, 0, :, 0:NGRP]
            first_of(group_hot, lg_g, g_max, NGRP, rt[:, 3, :, 0:NGRP])
            grp4 = [P, NT, NGRP, EPG]
            hot4 = group_hot.unsqueeze(3).to_broadcast(grp4)
            in_group = rt[:, 4, :, :]
            v4 = in_group.rearrange("p a (g e) -> p a g e", g=NGRP)
            masked, masked2 = rt[:, 5, :, :], rt[:, 6, :, :]
            for t in range(NT):
                ins = dve.tensor_copy(v4[:, t], hot4[:, t])
                ins.then_inc(r_step, 1)
                steps[0] += 1
            dve.wait_ge(r_step, steps[0])
            then_step(dve.tensor_tensor(masked, lg_e, in_group, ALU.mult))
            then_step(dve.tensor_scalar(in_group, in_group, BIG, -BIG, ALU.mult, ALU.add))
            then_step(dve.tensor_tensor(masked, masked, in_group, ALU.add))
            hot1, hot2 = rt[:, 7, :, :], rt[:, 8, :, :]
            then_step(dve.tensor_reduce(m1, masked, AX_X, ALU.max))
            first_of(hot1, masked, m1, NEXP, rt[:, 3, :, :])
            then_step(dve.scalar_tensor_tensor(out=masked2, in0=hot1, scalar=-2 * BIG, in1=masked,
                                               op0=ALU.mult, op1=ALU.add))
            then_step(dve.tensor_reduce(g_w, masked2, AX_X, ALU.max))
            dve.tensor_tensor(d21, g_w, m1, ALU.subtract).then_inc(exp_in, 1)
            first_of(hot2, masked2, g_w, NEXP, rt[:, 3, :, :])
            dve.tensor_tensor(rt[:, 9, :, :], hot1, hot2, ALU.add).then_inc(mask_done, 1)
            dve.wait_ge(exp_done, 2)
            dve.wait_ge(mask_done, 1)
            then_step(dve.tensor_reduce(g_sum, rt[:, 2, :, 0:NGRP], AX_X, ALU.add))
            then_step(dve.reciprocal(g_w, g_sum))
            then_step(dve.tensor_scalar(w1, e21, 1.0, None, ALU.add))
            then_step(dve.reciprocal(w1, w1))
            then_step(dve.tensor_tensor(w1, w1, g_w, ALU.mult))
            then_step(dve.tensor_tensor(g_w, w1, e21, ALU.mult))
            then_step(dve.tensor_tensor(hot1, hot1, bc(w1, NEXP), ALU.mult))
            then_step(dve.tensor_tensor(hot2, hot2, bc(g_w, NEXP), ALU.mult))
            then_step(dve.tensor_tensor(weight_of[:, :, :], hot1, hot2, ALU.add))
            mask = rt[:, 9, :, :]
            off = rt[:, 10, :, :]
            then_step(dve.tensor_scalar(off, mask, -1000.0, 1000.0, ALU.mult, ALU.add))
            dve.wait_ge(ranks_ps, 1)
            then_step(dve.tensor_tensor(rank_of[:, :, :], off, R[:, 0:NT * NEXP].rearrange("p (a e) -> p a e", a=NT),
                                        ALU.add))
            dve.tensor_copy(count_i[:, :], R[:, 128:128 + NEXP]).then_inc(counts_ready, 1)

            def extras():
                n_x, run = rt[:, 0, 0, :], [rt[:, 1, 0, :], rt[:, 2, 0, :]]
                then_step(dve.memset(n_x, 0.0))
                for p in range(1, MAXP):
                    then_step(dve.scalar_tensor_tensor(out=n_x, in0=R[:, 128:128 + NEXP], scalar=float(CAP * p),
                                                       in1=n_x, op0=ALU.is_gt, op1=ALU.add))
                then_step(dve.tensor_copy(extra_i[:, :], n_x))
                then_step(dve.memset(run[0], 0.0))
                then_step(dve.tensor_copy(run[0][:, 1:NEXP], n_x[:, 0:NEXP - 1]))
                shift, a = 1, 0
                while shift < NEXP:
                    then_step(dve.tensor_copy(run[1 - a], run[a]))
                    then_step(dve.tensor_tensor(run[1 - a][:, shift:NEXP], run[a][:, shift:NEXP],
                                                run[a][:, 0:NEXP - shift], ALU.add))
                    shift, a = 2 * shift, 1 - a
                dve.tensor_copy(extra_before_i[:, :], run[a]).then_inc(extra_ready, 1)

            def run_pass(s, n, q, e, g):
                iota = iota_cap
                if s is extra:
                    iota = iota_pass
                    dve.tensor_scalar(iota_pass[:, :], iota_pass[:, :], float(CAP), None, ALU.add
                                      ).then_inc(iota_moved, 1)
                    dve.wait_ge(iota_moved, n + 1)
                for t in range(NT):
                    rank = rank_of[:, t, bass.ds(e, 1)]
                    dve.tensor_scalar(sel[:, t, :], iota[:, :], rank, rstd_h[:, t:t + 1], ALU.is_equal, ALU.mult)
                    dst = scat[:, t, q * CAP:(q + 1) * CAP] if s is first else scat_x[:, t, :]
                    ins = dve.tensor_scalar(dst, iota[:, :], rank, weight_of[:, t, bass.ds(e, 1)],
                                            ALU.is_equal, ALU.mult)
                ins.then_inc(s.sel, 1)
                dve.wait_ge(s.xeT_ps, n + 1)
                dve.tensor_tensor(xeT[:, :, :, :], TR[:, :].rearrange("p (b j c) -> p b j c", b=KC, j=NQ),
                                  g_ffn.rearrange("p (j b) -> p b j", b=KC).unsqueeze(3).to_broadcast([P, KC, NQ, CAP]),
                                  ALU.mult).then_inc(s.xeT, 1)
                dve.wait_ge(s.silu, n + 1)
                dve.tensor_tensor(hT[:, :, :], silu_g[:, :, :],
                                  TR[:, 0:256].rearrange("p (b c) -> p b c", b=2)[:, :, 2 * CAP:4 * CAP],
                                  ALU.mult).then_inc(s.hT, 1)

            def scatter(s, m):
                for t in range(NT):
                    for j in range(NB):
                        dve.wait_ge(s.scattered, NT * NB * m + NB * t + j + 1)
                        cols = slice(j * NBLK, (j + 1) * NBLK)
                        dve.tensor_tensor(acc[:, t, cols], O[j][:, :], acc[:, t, cols], ALU.add).then_inc(s.o_free, 1)

            extras()
            dve.wait_ge(acc_init, NT)
            def first_ranks():
                dve.tensor_copy(iota_pass[:, :], iota_cap[:, :])
                dve.drain()

            experts(dve, run_pass, scatter, after_extra=lambda: dve.sem_inc(extras_over, 1),
                    before_extra=first_ranks)

            dve.wait_ge(final_in, 16)
            for t in range(NT):
                dve.wait_ge(rms_o_done, t + 1)
                dve.reciprocal(rstd_o[:, t:t + 1], rms_o[:, t:t + 1]).then_inc(rstd_o_done, 1)
                dve.wait_ge(rstd_o_done, t + 1)
                for j in range(2):
                    cols = slice(j * D // 2, (j + 1) * D // 2)
                    dve.scalar_tensor_tensor(out=acc[:, t, cols], in0=acc[:, t, cols], scalar=rstd_o[:, t:t + 1],
                                             in1=g_final[:, cols], op0=ALU.mult, op1=ALU.mult).then_inc(out_ready, 1)

        @block.tensor
        def _(pe):
            pe.wait_ge(consts, N_CONSTS)
            pe.wait_ge(cols_in, 16 * 3)
            pe.transpose(L[:, 0:2 * KD + GRP], col_rows[:, :], ident[0:2 * KD + GRP, 0:2 * KD + GRP]).then_inc(cols_ps, 1)
            for t in range(NT):
                pe.wait_ge(x_in[t], 16)
            for k in range(KD):
                if k >= 2:
                    pe.wait_ge(xt_lo, k - 1)
                for t in range(NT):
                    ins = pe.transpose(X[k % 2][:, t * P:(t + 1) * P], h[:, t, k * P:(k + 1) * P], ident[:, :])
                ins.then_inc(xt_ps, 1)

            def column_block(n, parity, ready=None, midway=None):
                for hc in range(HC):
                    pe.wait_ge(lo_done, HC * n + hc + 1)
                    for j in range(2):
                        k = 2 * hc + j
                        if ready is not None:
                            ready(k)
                        for t in range(NT):
                            toks = slice(t * P, (t + 1) * P)
                            for part, (a, b) in enumerate(((xT_hi, w_hi), (xT_hi, w_lo), (xT_lo, w_hi))):
                                ins = pe.matmul(Z[parity][t][:, :], a[:, k, toks], b[:, hc % 2, j, :],
                                                start=(k == 0 and part == 0), stop=(k == KD - 1 and part == 2))
                    ins.then_inc(w_used, 1)
                    if hc == HC // 2 - 1 and midway is not None:
                        midway()

            for n in range(NB + 2):
                if 2 <= n < NB + 2:
                    if n - 2 < NB:
                        pe.wait_ge(v_ready, NT * (n - 1))
                column_block(n, n % 2, (lambda k: pe.wait_ge(xt_lo, k + 1)) if n == 0 else None)
                if n == 1:
                    pe.wait_ge(ws_masked, 1)
                    for g in range(0, GRP, 2):
                        i = g // 2
                        if i >= 2:
                            pe.wait_ge(wst_done, i - 1)
                        for j in range(2):
                            ins = pe.transpose(X[i % 2][:, j * P:(j + 1) * P], ws_raw[:, g + j, :], ident[:, :])
                        ins.then_inc(wst_ps, 1)
            pe.wait_ge(wst_done, GRP // 2)
            pe.wait_ge(ln_done, NT * NB)
            for g in range(0, GRP, 2):
                for t in range(NT):
                    i = g + t
                    if i >= 2:
                        pe.wait_ge(sv_done, i - 1)
                    for j in range(2):
                        ins = pe.matmul(X[i % 2][:, j * GD:(j + 1) * GD], ws_T[:, g + j, :],
                                        v[:, t, (g + j) * GD:(g + j + 1) * GD], start=True, stop=True)
                    ins.then_inc(sv_ps, 1)
            for n in (NB + 2, NB + 3):
                pe.wait_ge(u_ready, NT * (n - NB - 1))
                column_block(n, n % 2)
            for i in range(KD // 2):
                pe.wait_ge(y_done, NT * (2 * i // 4 + 1))
                if i >= 2:
                    pe.wait_ge(yt_lo, i - 1)
                for j in range(2):
                    for t in range(NT):
                        ins = pe.transpose(X[i % 2][:, j * T + t * P:j * T + (t + 1) * P],
                                           v[:, t, (2 * i + j) * P:(2 * i + j + 1) * P], ident[:, :])
                ins.then_inc(yt_ps, 1)

            def router_block(b):
                pe.wait_ge(h_done, NT * (b + 1))
                for i in range(2):
                    if b:
                        pe.wait_ge(ht_done, 2 * (b - 1) + i + 1)
                    for j in range(2):
                        k = 4 * b + 2 * i + j
                        for t in range(NT):
                            ins = pe.transpose(X[i][:, j * T + t * P:j * T + (t + 1) * P],
                                               h[:, t, k * P:(k + 1) * P], ident[:, :])
                    ins.then_inc(ht_ps, 1)

            for b in range(NB):
                n = 2 * NB + b
                if b < 2:
                    pe.wait_ge(u_ready, NT * (b + 3))
                else:
                    pe.wait_ge(h_done, NT * (b - 1))
                column_block(n, b % 2, (lambda k: pe.wait_ge(yt_lo, k // 2 + 1)) if b == 0 else None,
                             (lambda: router_block(b - 1)) if b else None)
            router_block(NB - 1)
            pe.wait_ge(router_in, 16 * 4)
            for t in range(NT):
                for k in range(KD):
                    pe.wait_ge(ht_done, k // 2 + 1)
                    ins = pe.matmul(L[:, 64 * t:64 * t + NR], hgT[:, k, t * P:(t + 1) * P], w_router[:, k, :],
                                    start=(k == 0), stop=(k == KD - 1))
            ins.then_inc(logits_ps, 1)
            pe.wait_ge(mask_done, 1)
            mask = rt[:, 9, :, :]
            pe.matmul(R[:, 0:NEXP], before[:, :], mask[:, 0, :], start=True, stop=True)
            pe.matmul(R[:, NEXP:2 * NEXP], ones[:, :], mask[:, 0, :], start=True, stop=False)
            pe.matmul(R[:, NEXP:2 * NEXP], before[:, :], mask[:, 1, :], start=False, stop=True)
            pe.matmul(R[:, 128:128 + NEXP], ones[:, :], mask[:, 0, :], start=True, stop=False)
            pe.matmul(R[:, 128:128 + NEXP], ones[:, :], mask[:, 1, :], start=False, stop=True).then_inc(ranks_ps, 1)

            def run_pass(s, n, q, e, g):
                is_first = s is first
                pe.wait_ge(s.sel, n + 1)
                for t in range(NT):
                    for j in range(NB):
                        ins = pe.matmul(XE[j * CAP:(j + 1) * CAP, :], sel[:, t, :],
                                        h[:, t, j * NBLK:(j + 1) * NBLK], start=(t == 0), stop=(t == NT - 1))
                ins.then_inc(s.xe_ps, 1)
                pe.wait_ge(s.xe, n + 1)
                for b in range(KC):
                    ins = pe.transpose(TR[:, b * P:(b + 1) * P], xe[:, b * P:(b + 1) * P], ident[:, :])
                ins.then_inc(s.xeT_ps, 1)
                pe.wait_ge(s.xeT, n + 1)
                for kc in range(FT):
                    if is_first:
                        pe.wait_ge(chunk_in[2 * kc], 16 * (n + 1))
                        pe.wait_ge(chunk_in[2 * kc + 1], 16 * (n + 1))
                    for kk in range(KC):
                        for c in range(NQ):
                            half = kk * FE + (c % 2) * 256
                            ins = pe.matmul(GU[c * CAP:(c + 1) * CAP, 0:256], xeT[:, kk, kc, :],
                                            ring[:, 2 * kc + c // 2, half:half + 256],
                                            start=(kc == 0 and kk == 0), stop=(kc == FT - 1 and kk == KC - 1))
                    if is_first and kc < FT - 1:
                        ins.then_inc(chunk_used, 2)
                ins.then_inc(s.gu_ps, 1)
                if is_first and q == NQ - 1:
                    transpose_scat(first)
                pe.wait_ge(s.gu, n + 1)
                for b in range(2):
                    ins = pe.transpose(TR[:, b * P:(b + 1) * P], gu[:, b * P:(b + 1) * P], ident[:, :])
                ins.then_inc(s.tr_ps, 1)
                pe.wait_ge(s.hT, n + 1)
                for f in range(FT):
                    if is_first:
                        pe.wait_ge(chunk_in[8 + f], 16 * (n + 1))
                    for j in range(NB):
                        ins = pe.matmul(Y[j * CAP:(j + 1) * CAP, :], hT[:, f % 2, (f // 2) * CAP:(f // 2 + 1) * CAP],
                                        ring[:, 8 + f, j * NBLK:(j + 1) * NBLK], start=(f == 0), stop=(f == FT - 1))
                    if is_first and f < FT - 1:
                        ins.then_inc(chunk_used, 1)
                ins.then_inc(s.y_ps, 1)
                if not is_first:
                    transpose_scat(extra)

            def transpose_scat(s):
                for t in range(NT):
                    if s is first:
                        ins = pe.transpose(XE[:, t * P:(t + 1) * P], scat[:, t, :], ident[:, :])
                    else:
                        ins = pe.transpose(XE[0:CAP, t * P:(t + 1) * P], scat_x[:, t, :], ident[:, :])
                ins.then_inc(s.scat_ps, 1)

            def scatter(s, m):
                a, b = (scatT, y) if s is first else (scatT_x, y_x)
                pe.wait_ge(s.scatT, m + 1)
                pe.wait_ge(s.y, NQ * (m + 1) if s is first else m + 1)
                for t in range(NT):
                    for j in range(NB):
                        pe.wait_ge(s.o_free, NT * NB * m + NB * t + j + 1)
                        pe.matmul(O[j][:, :], a[:, t, :], b[:, j * NBLK:(j + 1) * NBLK],
                                  start=True, stop=True).then_inc(s.scattered, 1)

            pe.wait_ge(counts_ready, 1)
            experts(pe, run_pass, scatter, at_start=lambda: pe.sem_inc(no_more_passes, 1),
                    after_extra=lambda: pe.sem_inc(no_more_passes, 1))


_INS = ["x", "norm_mix", "norm_ffn", "norm_final", "a_w_in", "a_ln_g", "a_ln_b", "a_w_s", "a_b_s", "a_w_out",
        "r_w_group", "r_b_group", "r_w_exp", "r_b_exp", "e_w_gate", "e_w_up", "e_w_down"]


def kernel(**inputs):
    import numpy as _np
    import concourse.bacc as _bacc
    from concourse.bass_utils import run_bass_kernel_spmd as _run

    nc = _bacc.Bacc("TRN2", target_bir_lowering=False, num_devices=1)
    arrays, args = {}, []
    for name in _INS:
        a = _np.ascontiguousarray(inputs[name])
        arrays[f"in_{name}"] = a
        args.append(nc.dram_tensor(f"in_{name}", a.shape, mybir.dt.from_np(a.dtype), kind="ExternalInput").ap())
    out = nc.dram_tensor("out_h", inputs["x"].shape, F32, kind="ExternalOutput").ap()
    hybrid_layer(nc, *args, out)
    r = _run(nc, [arrays], core_ids=[0])
    return r.results[0]["out_h"]
```

```python
from contextlib import ExitStack

import concourse.bass as bass
from concourse import mybir

F32 = mybir.dt.float32
F32R = mybir.dt.float32r
I32 = mybir.dt.int32
BF16 = mybir.dt.bfloat16
ALU = mybir.AluOpType
ACT = mybir.ActivationFunctionType
AX_X = mybir.AxisListType.X

P = 128
EPS = 1e-6
CAP = 32
BIG = 1.0e30


def hybrid_layer(nc, x, norm_mix, norm_ffn, norm_final, w_in, ln_g, ln_b, w_s, b_s, w_out,
                 r_w_group, r_b_group, r_w_exp, r_b_exp, e_gate, e_up, e_down, out):
    _, T, D = x.shape
    NT = T // P
    KD = D // P
    NBLK = 512
    NB = D // NBLK
    GRP = w_s.shape[1]
    GD = D // GRP
    NGRP = r_w_group.shape[2]
    NEXP = r_w_exp.shape[2]
    EPG = NEXP // NGRP
    NR = NGRP + NEXP
    FE = e_gate.shape[3]
    FT = FE // P
    NC = 12
    KC = 4
    NSGL = 6
    HC = 8
    NQ = P // CAP
    MAXP = T // CAP
    assert (NT, KD, NB, FT, NQ, GD, NGRP * EPG) == (2, 16, 4, 4, 4, 256, NEXP)

    with ExitStack() as ctx:
        def sem(name):
            return ctx.enter_context(nc.semaphore(name))

        def sb(name, shape, dt=F32, stack=ctx):
            return stack.enter_context(nc.sbuf_tensor(name, shape, dt))

        ring = sb("ring", [P, NC, 2048])
        h = sb("h", [P, NT, D])
        v = sb("v", [P, NT, D])
        ident = sb("ident", [P, P])
        iota_cap = sb("iota_cap", [P, CAP])
        before = sb("before", [P, P], BF16)
        ones_bf = sb("ones_bf", [P, P], BF16)
        ones = sb("ones", [P, P])
        w_router = sb("w_router", [P, KD, NR])
        b_router = sb("b_router", [P, NR])
        col_rows = sb("col_rows", [2 * KD + GRP, P])
        cols_T = sb("cols_T", [P, 2 * KD + GRP])
        g_mix, g_ffn, bias_s = cols_T[:, 0:KD], cols_T[:, KD:2 * KD], cols_T[:, 2 * KD:2 * KD + GRP]
        v_stats = sb("v_stats", [P, NT, NB, 6])
        v_mean_var = sb("v_mean_var", [P, NT, 2])
        rows = sb("rows", [P, 12, NT])
        unused_col = rows[:, 11, 0:1]
        sumsq_h = sb("sumsq_h", [P, NT, NB])
        sumsq_o = sb("sumsq_o", [P, NT, NB])
        eps_col = sb("eps_col", [P, 1])
        iota_e = sb("iota_e", [P, NT, NEXP])
        mask = sb("mask", [P, NT, NEXP], BF16)
        rank_of = sb("rank_of", [P, NT, NEXP])
        weight_of = sb("weight_of", [P, NT, NEXP])
        count_f = sb("count_f", [P, NEXP])
        count_i = sb("count_i", [P, NEXP], I32)
        extra_i = sb("extra_i", [P, NEXP], I32)
        extra_before_i = sb("extra_before_i", [P, NEXP], I32)
        rstd_x, rms_x, ssq_x, rstd_v, std_v = (rows[:, i, :] for i in range(5))
        rstd_h, rms_h, ssq_h, rstd_o, rms_o, ssq_o = (rows[:, i, :] for i in range(5, 11))

        with ExitStack() as mixer:
            xT_hi = sb("xT_hi", [P, KD, T], F32R, mixer)
            xT_lo = sb("xT_lo", [P, KD, T], F32R, mixer)
            w_raw = sb("w_raw", [P, 4, 2, NBLK], F32, mixer)
            w_hi = sb("w_hi", [P, 2, 2, NBLK], F32R, mixer)
            w_lo = sb("w_lo", [P, 2, 2, NBLK], F32R, mixer)
            u = sb("u", [P, 2, NT, NBLK], F32, mixer)
            h_T = u[:, 0, :, :].rearrange("p a (b t) -> p (a b) t", t=T)
            square = u[:, 1, :, :]
        acc = sb("acc", [P, NT, D])
        late = sb("late", [P, 4, 2048])
        y = sb("y", [P, D])
        xeT = sb("xeT", [P, KC, NQ, CAP])
        gu = sb("gu", [P, 256])
        silu_g = sb("silu_g", [P, 2, 2 * CAP])
        hT = sb("hT", [P, 2, 2 * CAP])
        scatT = sb("scatT", [P, NT, P])
        scatT_x = sb("scatT_x", [CAP, NT, P])
        scat = sb("scat", [P, NT, P])
        scat_x = sb("scat_x", [P, NT, CAP])
        sel = sb("sel", [P, NT, CAP])
        iota_pass = sb("iota_pass", [P, CAP])
        with ExitStack() as router:
            lg = sb("lg", [P, NT, NR], F32, router)
            rt = sb("rt", [P, 10, NT, NEXP], F32, router)
            rc = sb("rc", [P, 9, NT], F32, router)
            rx = sb("rx", [P, 4, NEXP], F32, router)
        (g_max, g_sum, m1, m2, d21, e21, w1, w2, column) = (rc[:, i, :] for i in range(9))
        group_hot, g_shifted, g_exp, g_scratch = (rt[:, i, :, 0:NGRP] for i in range(4))
        masked, masked2, hot1, hot2, off, e_scratch = (rt[:, i, :, :] for i in range(4, 10))
        y_x = sb("y_x", [CAP, D])
        xe = w_router[:, :, :].rearrange("p k n -> p (k n)")[:, 0:NBLK]
        g_final = ring[:, NSGL, :]

        ws_raw = ring[:, 9, 0:GRP * P].rearrange("p (g s) -> p g s", g=GRP)
        ws_T = ring[:, 9, GRP * P:2 * GRP * P].rearrange("p (g s) -> p g s", g=GRP)
        g_ln, b_ln = ring[:, 10, :], ring[:, 11, :]

        bank = [ctx.enter_context(nc.psum_tensor(f"bank{i}", [P, NBLK], F32)) for i in range(8)]
        Z = [[bank[0], bank[1]], [bank[2], bank[3]]]
        X = bank[4:8]
        L = bank[6:8]
        R = bank[4]
        COUNTS = slice(128, 128 + NEXP)
        O = bank[0:4]
        XE, GU, TR, Y = bank[4], bank[5], bank[6], bank[7]

        x_in = [sem(f"x_in{q}") for q in range(NB)]
        raw_in = [sem(f"raw_in{s}") for s in range(4)]
        chunk_in = [sem(f"chunk_in{c}") for c in range(NC)]
        chunk_in_odd = {c: sem(f"chunk_in_odd{c}") for c in range(NSGL, NC)}
        cols_in, cols_ps, cols_done = sem("cols_in"), sem("cols_ps"), sem("cols_done")
        ws_in, router_in, ln_in, final_in = sem("ws_in"), sem("router_in"), sem("ln_in"), sem("final_in")
        consts, ws_masked = sem("consts"), sem("ws_masked")
        xt_ps, xt_hi, xt_lo = sem("xt_ps"), sem("xt_hi"), sem("xt_lo")
        hi_done, lo_done, w_used = sem("hi_done"), sem("lo_done"), sem("w_used")
        v_ready, u_ready, y_done = sem("v_ready"), sem("u_ready"), sem("y_done")
        ln_step, ln_done, var_done, std_done = sem("ln_step"), sem("ln_done"), sem("var_done"), sem("std_done")
        wst_ps, wst_done = sem("wst_ps"), sem("wst_done")
        sv_ps, sv_done = sem("sv_ps"), sem("sv_done")
        yt_ps, yt_hi, yt_lo = sem("yt_ps"), sem("yt_hi"), sem("yt_lo")
        sumsq_x_done, rms_x_done, rstd_x_done = sem("sumsq_x_done"), sem("rms_x_done"), sem("rstd_x_done")
        h_done, sumsq_h_done = sem("h_done"), sem("sumsq_h_done")
        ht_ps, ht_act, ht_dve = sem("ht_ps"), sem("ht_act"), sem("ht_dve")
        router_w_ready, count_f_ready = sem("router_w_ready"), sem("count_f_ready")
        ssq_h_done, rms_h_done = sem("ssq_h_done"), sem("rms_h_done")
        logits_ps, mask_done, ranks_ps, exp_in, exp_done = (
            sem("logits_ps"), sem("mask_done"), sem("ranks_ps"), sem("exp_in"), sem("exp_done"))
        r_step, counts_ready, extra_ready, p_step = (
            sem("r_step"), sem("counts_ready"), sem("extra_ready"), sem("p_step"))
        acc_init, iota_moved = sem("acc_init"), sem("iota_moved")
        w1_done, w2_done, weights_ready = sem("w1_done"), sem("w2_done"), sem("weights_ready")
        extras_over = sem("extras_over")
        chunk_used, no_more_passes = sem("chunk_used"), sem("no_more_passes")
        out_ready_act, acc_g_done = sem("out_ready_act"), sem("acc_g_done")
        ssq_o_done, ssq_o_sum, rms_o_done, rstd_o_done, out_ready, out_stored = (
            sem("ssq_o_done"), sem("ssq_o_sum"), sem("rms_o_done"), sem("rstd_o_done"), sem("out_ready"), sem("out_stored"))

        class PassSems:

            def __init__(self, s):
                self.sel = sem(f"sel_ready{s}")
                self.xe_ps = sem(f"xe_ps{s}")
                self.xe = sem(f"xe_ready{s}")
                self.xeT_ps = sem(f"xeT_ps{s}")
                self.xeT = sem(f"xeT_ready{s}")
                self.gu_ps = sem(f"gu_ps{s}")
                self.gu = sem(f"gu_ready{s}")
                self.tr_ps = sem(f"tr_ps{s}")
                self.silu = sem(f"silu_ready{s}")
                self.hT = sem(f"hT_ready{s}")
                self.y_ps = sem(f"y_ps{s}")
                self.y = sem(f"y_ready{s}")
                self.scat_ps = sem(f"scat_ps{s}")
                self.scatT = sem(f"scatT_ready{s}")
                self.scattered = sem(f"scattered{s}")
                self.o_free = sem(f"o_free{s}")

        first, extra = PassSems(""), PassSems("_x")

        def adds_done(n_scatters):
            return n_scatters * NT * NB + NB

        def w_in_half(col, hc):
            return w_in[0, hc * 2 * P:(hc + 1) * 2 * P, bass.ds(col, NBLK)].rearrange("(j p) n -> p j n", p=P)

        def w_out_half(col, hc):
            return w_out[0, hc * 2 * P:(hc + 1) * 2 * P, col:col + NBLK].rearrange("(j p) n -> p j n", p=P)

        def expert_chunk(e, c):
            if c < 8:
                w, k = (e_gate, e_up)[c % 2], c // 2
                return w[0, e, k * KC * P:(k + 1) * KC * P, :].rearrange("(j p) n -> p j n", p=P)
            return e_down[0, e, (c - 8) * P:(c - 7) * P, :]

        def slot_of(c, odd):
            if odd and c >= NSGL:
                return v[:, c - NSGL, :] if c < NSGL + NT else late[:, (c - NSGL) % 4, :]
            return ring[:, c, :]

        def load_chunk(sp, e, c, odd):
            dst = slot_of(c, odd)
            if c < 8:
                dst = dst.rearrange("p (j n) -> p j n", j=KC)
            sp.dma_start(dst, expert_chunk(e, c)).then_inc((chunk_in_odd if odd and c >= NSGL else chunk_in)[c], 16)

        def wait_chunk(pe, c, g, q):
            if c < NSGL:
                pe.wait_ge(chunk_in[c], 16 * (NQ * g + q + 1))
            else:
                pe.wait_ge((chunk_in, chunk_in_odd)[q % 2][c], 16 * (NQ // 2 * g + q // 2 + 1))

        def experts(eng, run_pass, scatter, after_extra, at_start=None, before_extra=None, last_scatter=None):

            def group(g, scatter_group):
                for q in range(NQ):
                    e = NQ * g + q
                    count = eng.value_load(count_i[0:1, bass.ds(e, 1)], min_val=0, max_val=T)
                    if at_start is not None:
                        with eng.If(count <= CAP):
                            at_start()
                        with eng.Else():
                            eng.nop()
                    run_pass(first, e, q, e, g)
                    with eng.If(count > CAP):
                        eng.wait_ge(extra_ready, 1)
                        eng.wait_ge(first.y, NB * (e + 1))
                        eng.wait_ge(first.o_free, NT * NB * g + NB)
                        n_extra = eng.value_load(extra_i[0:1, bass.ds(e, 1)], min_val=1, max_val=MAXP - 1)
                        n_before = eng.value_load(extra_before_i[0:1, bass.ds(e, 1)], min_val=0,
                                                  max_val=T * 2 // CAP)
                        if before_extra is not None:
                            before_extra()
                        with eng.Fori(0, n_extra) as i:
                            run_pass(extra, n_before + i, q, e, g)
                            scatter(extra, n_before + i)
                        eng.wait_ge(extra.o_free, adds_done(n_before + n_extra))
                        after_extra()
                    with eng.Else():
                        eng.nop()
                scatter_group(first, g)

            n_groups = NEXP // NQ
            with eng.Fori(0, n_groups if last_scatter is None else n_groups - 1) as g:
                group(g, scatter)
            if last_scatter is not None:
                group(n_groups - 1, last_scatter)

        block = ctx.enter_context(nc.Block())

        @block.sync
        def _(sp):
            def load_half(src, n, hc, fresh=False):
                if not fresh:
                    sp.wait_ge(lo_done, HC * n + hc - 3)
                sp.dma_start(w_raw[:, hc % 4, :, :], src).then_inc(raw_in[hc % 4], 16)

            for q in range(NB):
                cols = slice(q * NBLK, (q + 1) * NBLK)
                sp.dma_start(h[:, :, cols], x[0, :, cols].rearrange("(t p) d -> p t d", p=P)).then_inc(x_in[q], 16)
                load_half(w_in_half(D, q), 0, q, fresh=True)
            for n in range(2 * NB):
                col = D + n * NBLK if n < NB else (n - NB) * NBLK
                for hc in range(4 if n == 0 else 0, HC):
                    load_half(w_in_half(col, hc), n, hc)
                load_chunk(sp, 0, n, False)
            for n in range(NB):
                for hc in range(HC):
                    load_half(w_out_half(n * NBLK, hc), 2 * NB + n, hc)
                c = 2 * NB + n
                if c == 9:
                    sp.wait_ge(sv_ps, NT * GRP // 2)
                if c == 10:
                    sp.wait_ge(ln_done, NT * NB)
                load_chunk(sp, 0, c, False)
                if n in (1, 2):
                    if n == 1:
                        sp.wait_ge(yt_ps, KD // 2)
                    load_chunk(sp, 1, NSGL + n - 1, True)

            def load_expert(e, odd, chunks):
                for c in chunks:
                    if c == 0:
                        sp.wait_ge(no_more_passes, e)
                    if c < NSGL:
                        sp.wait_ge(chunk_used, (NSGL // 2) * (e - 1) + c // 2 + 1)
                    load_chunk(sp, e, c, odd)

            sp.wait_ge(lo_done, 3 * NB * HC)
            load_expert(1, True, range(NSGL + NT, NC - 2))
            sp.wait_ge(w_used, 3 * NB * HC)
            load_expert(1, True, range(NC - 2, NC))
            load_expert(1, True, range(NSGL))
            with sp.Fori(1, NEXP // 2) as m:
                load_expert(2 * m, False, range(NC))
                load_expert(2 * m + 1, True, range(NC))
            sp.wait_ge(first.gu_ps, NEXP - 1)
            sp.dma_start(g_final, norm_final.rearrange("(a d) -> a d", a=1).partition_broadcast(P)
                         ).then_inc(final_in, 16)

            for t in range(NT):
                for j in range(2):
                    sp.wait_ge((out_ready, out_ready_act)[j], t + 1)
                    cols = slice(j * D // 2, (j + 1) * D // 2)
                    sp.dma_start(out[0, t * P:(t + 1) * P, cols], acc[:, t, cols]).then_inc(out_stored, 16)
            sp.wait_ge(out_stored, 16 * NT * 2)

        @block.gpsimd
        def _(pool):
            pool.memset(ones[:, :], 1.0).then_inc(p_step, 1)
            pool.memset(eps_col[:, :], EPS).then_inc(consts, 1)
            pool.wait_ge(p_step, 1)
            pool.affine_select(out=ident[:, :], in_=ones[:, :], compare_op=ALU.is_equal, fill=0.0, base=0,
                               pattern=[[-1, P]], channel_multiplier=1).then_inc(consts, 1)
            pool.wait_ge(lo_done, HC // 2)
            pool.dma_start(ws_raw, w_s[0].rearrange("g t s -> t g s")).then_inc(ws_in, 16)
            pool.dma_start(w_router[:, :, 0:NGRP], r_w_group[0].rearrange("(k p) n -> p k n", p=P)).then_inc(router_in, 16)
            pool.dma_start(w_router[:, :, NGRP:NR], r_w_exp[0].rearrange("(k p) n -> p k n", p=P)).then_inc(router_in, 16)
            pool.dma_start(b_router[:, 0:NGRP], r_b_group.partition_broadcast(P)).then_inc(router_in, 16)
            pool.dma_start(b_router[:, NGRP:NR], r_b_exp.partition_broadcast(P)).then_inc(router_in, 16)
            pool.wait_ge(lo_done, HC)
            pool.dma_start(g_ln, ln_g.partition_broadcast(P)).then_inc(ln_in, 16)
            pool.dma_start(b_ln, ln_b.partition_broadcast(P)).then_inc(ln_in, 16)
            pool.affine_select(out=before[:, :], in_=ones[:, :], compare_op=ALU.is_gt, fill=0.0, base=0,
                               pattern=[[1, P]], channel_multiplier=-1).then_inc(consts, 1)
            pool.memset(ones_bf[:, :], 1.0).then_inc(consts, 1)
            pool.iota(iota_cap[:, :], pattern=[[1, CAP]], base=0, channel_multiplier=0,
                      allow_small_or_imprecise_dtypes=True).then_inc(consts, 1)
            pool.iota(iota_e[:, :, :], pattern=[[0, NT], [1, NEXP]], base=0, channel_multiplier=0,
                      allow_small_or_imprecise_dtypes=True).then_inc(consts, 1)
            pool.wait_ge(router_in, 16 * 4)
            pool.wait_ge(cols_done, 1)
            pool.tensor_tensor(w_router[:, :, :], w_router[:, :, :], g_ffn.unsqueeze(2).to_broadcast([P, KD, NR]),
                               ALU.mult).then_inc(router_w_ready, 1)
            pool.wait_ge(ws_in, 16)
            pool.affine_select(out=ws_raw, in_=ws_raw, compare_op=ALU.is_ge, fill=0.0, base=0,
                               pattern=[[0, GRP], [-1, P]], channel_multiplier=1).then_inc(ws_masked, 1)
            pool.wait_ge(w1_done, 1)
            pool.tensor_tensor(w2, w1, e21, ALU.mult).then_inc(w2_done, 1)
            pool.tensor_tensor(hot1, hot1, w1.unsqueeze(2).to_broadcast([P, NT, NEXP]), ALU.mult).then_inc(w2_done, 1)
            pool.wait_ge(w2_done, 2)
            pool.tensor_tensor(hot2, hot2, w2.unsqueeze(2).to_broadcast([P, NT, NEXP]), ALU.mult).then_inc(w2_done, 1)
            pool.wait_ge(w2_done, 3)
            pool.tensor_tensor(weight_of[:, :, :], hot1, hot2, ALU.add).then_inc(weights_ready, 1)
            steps = [1]

            def then_step(ins):
                ins.then_inc(p_step, 1)
                steps[0] += 1
                pool.wait_ge(p_step, steps[0])

            n_x, above, run = rx[:, 0, :], rx[:, 1, :], [rx[:, 2, :], rx[:, 3, :]]
            pool.wait_ge(count_f_ready, 1)
            then_step(pool.memset(n_x, 0.0))
            for p in range(1, MAXP):
                then_step(pool.tensor_scalar(above, count_f[:, :], float(CAP * p), None, ALU.is_gt))
                then_step(pool.tensor_tensor(n_x, n_x, above, ALU.add))
            then_step(pool.tensor_copy(extra_i[:, :], n_x))
            then_step(pool.memset(run[0], 0.0))
            then_step(pool.tensor_copy(run[0][:, 1:NEXP], n_x[:, 0:NEXP - 1]))
            shift, a = 1, 0
            while shift < NEXP:
                then_step(pool.tensor_copy(run[1 - a], run[a]))
                then_step(pool.tensor_tensor(run[1 - a][:, shift:NEXP], run[a][:, shift:NEXP],
                                             run[a][:, 0:NEXP - shift], ALU.add))
                shift, a = 2 * shift, 1 - a
            pool.tensor_copy(extra_before_i[:, :], run[a]).then_inc(extra_ready, 1)

        IDENT_READY, ALL_CONSTS = 2, 6

        @block.scalar
        def _(act):
            act.dma_start(col_rows[0:KD, :], norm_mix.rearrange("a (k p) -> (a k) p", p=P)).then_inc(cols_in, 16)
            act.dma_start(col_rows[KD:2 * KD, :], norm_ffn.rearrange("a (k p) -> (a k) p", p=P)).then_inc(cols_in, 16)
            act.dma_start(col_rows[2 * KD:2 * KD + GRP, :], b_s[0]).then_inc(cols_in, 16)
            def hi_half(n, hc, fresh=False):
                if not fresh:
                    act.wait_ge(w_used, HC * n + hc - 1)
                act.wait_ge(raw_in[hc % 4], 16 * (2 * n + hc // 4 + 1))
                act.copy(w_hi[:, hc % 2, :, :], w_raw[:, hc % 4, :, :]).then_inc(hi_done, 1)

            def gelu_block(n, parity, dst, done):
                act.wait_ge(w_used, HC * (n + 1))
                for t in range(NT):
                    act.activation(dst(t), Z[parity][t][:, :], ACT.Gelu_apprx_tanh,
                                   scale=rstd_x[:, t:t + 1]).then_inc(done, 1)

            def square_x(t):
                act.activation(v[:, t, :], h[:, t, :], ACT.Square, accum_out=ssq_x[:, t:t + 1]).then_inc(sumsq_x_done, 1)

            hi_half(0, 0, fresh=True)
            act.wait_ge(cols_ps, 1)
            act.copy(cols_T[:, :], Z[0][0][:, 0:2 * KD + GRP]).then_inc(cols_done, 1)
            act.wait_ge(cols_done, 1)
            for hc in range(HC):
                for k in (2 * hc, 2 * hc + 1):
                    act.wait_ge(xt_ps, k + 1)
                    act.activation(xT_hi[:, k, :], X[k % 4][:, 0:T], ACT.Copy, scale=g_mix[:, k:k + 1]
                                   ).then_inc(xt_hi, 1)
                if hc > 0:
                    hi_half(0, hc, fresh=hc < 2)
                if hc == HC - 2:
                    for q in range(NB):
                        act.wait_ge(x_in[q], 16)
                    square_x(0)
            square_x(1)
            hi_half(1, 0)
            hi_half(1, 1)
            act.wait_ge(sumsq_x_done, 2)
            act.activation(rms_x, ssq_x, ACT.Sqrt, scale=1.0 / D, bias=eps_col[:, :]).then_inc(rms_x_done, 1)
            hi_half(1, 2)
            act.wait_ge(rstd_x_done, 1)
            gelu_block(0, 0, lambda t: v[:, t, 0:NBLK], v_ready)
            for hc in range(3, HC):
                hi_half(1, hc)

            def v_block(n, parity):
                hi_half(n, 0)
                hi_half(n, 1)
                gelu_block(n - 1, parity, lambda t: v[:, t, bass.ds((n - 1) * NBLK, NBLK)], v_ready)
                for hc in range(2, HC):
                    hi_half(n, hc)

            for n in range(2, NB + 1):
                v_block(n, (n - 1) % 2)
            n = NB + 1
            hi_half(n, 0)
            hi_half(n, 1)
            gelu_block(n - 1, 0, lambda t: u[:, 0, t, :], u_ready)
            for i in range(GRP // 2):
                act.wait_ge(wst_ps, i + 1)
                act.copy(ws_T[:, 2 * i:2 * i + 2, :], X[i % 4][:, 0:2 * P].rearrange("p (g t) -> p g t", g=2)
                         ).then_inc(wst_done, 1)
            for hc in range(2, HC):
                hi_half(n, hc)
                if hc == 2:
                    act.wait_ge(var_done, NT)
                    act.activation(std_v, v_mean_var[:, :, 1], ACT.Sqrt, bias=eps_col[:, :]).then_inc(std_done, 1)
            n = NB + 2
            hi_half(n, 0)
            hi_half(n, 1)
            gelu_block(n - 1, 1, lambda t: u[:, 1, t, :], u_ready)

            def bias_v(i):
                g, t = i // NT * 2, i % NT
                act.wait_ge(sv_ps, i + 1)
                for j in range(2):
                    r = act.activation(v[:, t, (g + j) * GD:(g + j + 1) * GD], X[i % 4][:, j * GD:(j + 1) * GD],
                                       ACT.Identity, bias=bias_s[:, g + j:g + j + 1])
                r.then_inc(sv_done, 1)

            for hc in range(2, HC):
                hi_half(n, hc)
                bias_v(hc - 2)
            n = NB + 3
            hi_half(n, 0)
            bias_v(HC - 2)
            hi_half(n, 1)
            bias_v(HC - 1)
            act.wait_ge(y_done, NT)
            gelu_block(n - 1, 0, lambda t: u[:, 0, t, :], u_ready)

            def yT_hi(i):
                act.wait_ge(w_used, HC * (2 * NB - 1) + i + 1)
                act.wait_ge(yt_ps, i + 1)
                act.copy(xT_hi[:, 2 * i:2 * i + 2, :], X[i % 4][:, :].rearrange("p (k t) -> p k t", k=2)
                         ).then_inc(yt_hi, 1)

            for hc in range(2, HC):
                hi_half(n, hc)
                yT_hi(hc - 2)
            n = 2 * NB
            hi_half(n, 0)
            hi_half(n, 1)
            act.wait_ge(y_done, NT * 2)
            gelu_block(n - 1, 1, lambda t: u[:, 1, t, :], u_ready)
            for hc in range(2, HC):
                hi_half(n, hc)
                if hc == 2:
                    act.activation(unused_col, eps_col[:, :], ACT.Sqrt)
                if hc in (3, 4):
                    yT_hi(HC - 2 + hc - 3)

            def sumsq_block(b):
                for t in range(NT):
                    act.wait_ge(h_done, NT * b + t + 1)
                    act.activation(square[:, t, :], h[:, t, b * NBLK:(b + 1) * NBLK], ACT.Square,
                                   accum_out=sumsq_h[:, t, b:b + 1]).then_inc(sumsq_h_done, 1)

            def hT_first(b):
                act.wait_ge(ht_ps, 2 * b + 1)
                act.copy(h_T[:, 0:2, :], X[0][:, :].rearrange("p (k t) -> p k t", k=2)).then_inc(ht_act, 1)

            for b in range(NB - 1):
                n = 2 * NB + 1 + b
                for hc in range(HC):
                    hi_half(n, hc)
                    if hc == 2:
                        sumsq_block(b)
                    if hc == 5:
                        hT_first(b)
            sumsq_block(NB - 1)
            hT_first(NB - 1)
            act.wait_ge(ssq_h_done, 1)
            act.activation(rms_h, ssq_h, ACT.Sqrt, scale=1.0 / D, bias=eps_col[:, :]).then_inc(rms_h_done, 1)
            act.activation(unused_col, eps_col[:, :], ACT.Exp)
            for i in range(2):
                act.wait_ge(exp_in, i + 1)
                act.activation((g_exp, e21)[i], (g_shifted, d21)[i], ACT.Exp).then_inc(exp_done, 1)
                act.copy(acc[:, i, :], h[:, i, :]).then_inc(acc_init, 1)

            def run_pass(s, n, q, e, g):
                act.activation(unused_col, eps_col[:, :], ACT.Silu)
                act.wait_ge(s.xe_ps, n + 1)
                act.copy(xe, XE[:, :]).then_inc(s.xe, 1)
                act.wait_ge(s.gu_ps, n + 1)
                act.copy(gu[:, :], GU[:, 0:256]).then_inc(s.gu, 1)
                act.wait_ge(s.tr_ps, n + 1)
                act.activation(silu_g[:, :, :], TR[:, 0:256].rearrange("p (b c) -> p b c", b=2)[:, :, 0:2 * CAP],
                               ACT.Silu).then_inc(s.silu, 1)
                if s is first and q == NQ - 1:
                    act.wait_ge(s.scat_ps, g + 1)
                    act.copy(scatT[:, :, :], XE[:, 0:NT * P].rearrange("p (a t) -> p a t", a=NT)).then_inc(s.scatT, 1)
                act.wait_ge(s.y_ps, n + 1)
                dst = y[q * CAP:(q + 1) * CAP, :] if s is first else y_x[:, :]
                for j in range(NB):
                    act.copy(dst[:, j * NBLK:(j + 1) * NBLK], Y[j * CAP:(j + 1) * CAP, :]).then_inc(s.y, 1)

            def scatter(s, m):
                if s is extra:
                    act.wait_ge(s.scat_ps, m + 1)
                    act.copy(scatT_x[:, :, :], XE[0:CAP, 0:NT * P].rearrange("p (a t) -> p a t", a=NT)
                             ).then_inc(s.scatT, 1)

            act.wait_ge(counts_ready, 1)
            experts(act, run_pass, scatter, after_extra=lambda: act.sem_inc(extras_over, 1))

            def square_out(t, j):
                act.wait_ge(first.o_free, adds_done(NEXP // NQ - 1) + NB * t + j + 1)
                act.activation(ring[:, NSGL + 1 + t, j * NBLK:(j + 1) * NBLK], acc[:, t, j * NBLK:(j + 1) * NBLK],
                               ACT.Square, accum_out=sumsq_o[:, t, j:j + 1]).then_inc(ssq_o_done, 1)

            def scale_out(t):
                act.wait_ge(ssq_o_sum, t + 1)
                act.activation(rms_o[:, t:t + 1], ssq_o[:, t:t + 1], ACT.Sqrt, scale=1.0 / D,
                               bias=eps_col[:, :]).then_inc(rms_o_done, 1)
                act.wait_ge(rstd_o_done, t + 1)
                act.activation(acc[:, t, D // 2:D], h[:, t, D // 2:D], ACT.Copy, scale=rstd_o[:, t:t + 1]
                               ).then_inc(out_ready_act, 1)

            act.activation(unused_col, eps_col[:, :], ACT.Sqrt)
            for j in range(NB):
                square_out(0, j)
            square_out(1, 0)
            scale_out(0)
            for j in range(1, NB):
                square_out(1, j)
            scale_out(1)

        @block.vector
        def _(dve):
            dve.sem_inc(first.o_free, NB)
            dve.sem_inc(extra.o_free, NB)

            def lo_half(n, hc):
                dve.wait_ge(hi_done, HC * n + hc + 1)
                dve.tensor_tensor(w_lo[:, hc % 2, :, :], w_raw[:, hc % 4, :, :],
                                  w_hi[:, hc % 2, :, :].bitcast(F32), ALU.subtract).then_inc(lo_done, 1)

            lo_half(0, 0)
            dve.wait_ge(cols_done, 1)
            for hc in range(HC):
                for k in (2 * hc, 2 * hc + 1):
                    dve.wait_ge(xt_hi, k + 1)
                    dve.scalar_tensor_tensor(out=xT_lo[:, k, :], in0=X[k % 4][:, 0:T], scalar=g_mix[:, k:k + 1],
                                             in1=xT_hi[:, k, :].bitcast(F32), op0=ALU.mult, op1=ALU.subtract
                                             ).then_inc(xt_lo, 1)
                if hc > 0:
                    lo_half(0, hc)

            def v_block(n, x_scale=False):
                for hc in range(2):
                    lo_half(n, hc)
                if x_scale:
                    dve.wait_ge(rms_x_done, 1)
                    dve.reciprocal(rstd_x, rms_x).then_inc(rstd_x_done, 1)
                lo_half(n, 2)
                for t in range(NT):
                    dve.wait_ge(v_ready, NT * n - NT + t + 1)
                    dve.bn_stats(v_stats[:, t, bass.ds(n - 1, 1), :], v[:, t, bass.ds((n - 1) * NBLK, NBLK)]
                                 ).then_inc(ln_step, 1)
                for hc in range(3, HC):
                    lo_half(n, hc)

            v_block(1, x_scale=True)
            with dve.Fori(2, NB + 1) as n:
                v_block(n)
            n = NB + 1
            lo_half(n, 0)
            dve.wait_ge(ln_step, NT * NB)
            for t in range(NT):
                dve.bn_aggr(v_mean_var[:, t, :], v_stats[:, t, :, :].rearrange("p a b -> p (a b)")).then_inc(var_done, 1)
            lo_half(n, 1)
            lo_half(n, 2)
            dve.wait_ge(std_done, 1)
            dve.wait_ge(ln_in, 32)
            dve.reciprocal(rstd_v, std_v).then_inc(ln_step, 1)
            dve.wait_ge(ln_step, NT * NB + 1)

            def norm_v(i):
                t, b = i % NT, i // NT
                cols = slice(b * NBLK, (b + 1) * NBLK)
                dve.scalar_tensor_tensor(out=v[:, t, cols], in0=v[:, t, cols], scalar=v_mean_var[:, t, 0:1],
                                         in1=g_ln[:, cols], op0=ALU.subtract, op1=ALU.mult).then_inc(ln_step, 1)
                dve.wait_ge(ln_step, NT * NB + 2 + i)
                dve.scalar_tensor_tensor(out=v[:, t, cols], in0=v[:, t, cols], scalar=rstd_v[:, t:t + 1],
                                         in1=b_ln[:, cols], op0=ALU.mult, op1=ALU.add).then_inc(ln_done, 1)

            norm_v(0)
            for i in range(1, NT * NB - 2):
                lo_half(n, i + 2)
                norm_v(i)

            def gate_v(b):
                for t in range(NT):
                    dve.wait_ge(u_ready, NT * b + t + 1)
                    dve.wait_ge(sv_done, NT * (b + 1))
                    cols = slice(b * NBLK, (b + 1) * NBLK)
                    dve.tensor_tensor(v[:, t, cols], u[:, b % 2, t, :], v[:, t, cols], ALU.mult).then_inc(y_done, 1)

            n = NB + 2
            for hc in range(HC):
                lo_half(n, hc)
                if hc < 2:
                    norm_v(NT * NB - 2 + hc)
                if hc in (5, 7):
                    gate_v((hc - 5) // 2)

            def yT_lo(i):
                dve.wait_ge(yt_hi, i + 1)
                dve.tensor_tensor(xT_lo[:, 2 * i:2 * i + 2, :], X[i % 4][:, :].rearrange("p (k t) -> p k t", k=2),
                                  xT_hi[:, 2 * i:2 * i + 2, :].bitcast(F32), ALU.subtract).then_inc(yt_lo, 1)

            n = NB + 3
            for hc in range(HC):
                lo_half(n, hc)
                if hc == 3:
                    gate_v(2)
                if hc >= 2:
                    yT_lo(hc - 2)
            n = 2 * NB
            for hc in range(HC):
                lo_half(n, hc)
                if hc == 1:
                    gate_v(3)
                if hc in (3, 4):
                    yT_lo(HC - 2 + hc - 3)

            def hT_second(b):
                dve.wait_ge(ht_ps, 2 * b + 2)
                dve.tensor_copy(h_T[:, 2:4, :], X[1][:, :].rearrange("p (k t) -> p k t", k=2)
                                ).then_inc(ht_dve, 1)

            def add_x(b):
                dve.wait_ge(w_used, HC * (2 * NB + b + 1))
                for t in range(NT):
                    cols = slice(b * NBLK, (b + 1) * NBLK)
                    dve.tensor_tensor(h[:, t, cols], Z[b % 2][t][:, :], h[:, t, cols], ALU.add).then_inc(h_done, 1)

            for b in range(NB - 1):
                n = 2 * NB + 1 + b
                for hc in range(HC):
                    lo_half(n, hc)
                    if hc == 1:
                        add_x(b)
                    if hc == 5:
                        hT_second(b)
            add_x(NB - 1)
            hT_second(NB - 1)
            dve.wait_ge(sumsq_h_done, NT * NB)
            dve.tensor_reduce(ssq_h, sumsq_h[:, :, :], AX_X, ALU.add).then_inc(ssq_h_done, 1)
            dve.wait_ge(rms_h_done, 1)

            steps = [0]

            def then_step(ins):
                ins.then_inc(r_step, 1)
                steps[0] += 1
                dve.wait_ge(r_step, steps[0])

            def bc(ap, n):
                return ap.unsqueeze(2).to_broadcast([P, NT, n])

            def first_of(onehot, values, best, n, scratch):
                then_step(dve.tensor_tensor(scratch, values, bc(best, n), ALU.is_equal))
                then_step(dve.scalar_tensor_tensor(out=scratch, in0=scratch, scalar=-1000.0, in1=iota_e[:, :, 0:n],
                                                   op0=ALU.mult, op1=ALU.add))
                then_step(dve.tensor_reduce(column, scratch, AX_X, ALU.min))
                then_step(dve.tensor_tensor(onehot, scratch, bc(column, n), ALU.is_equal))

            then_step(dve.reciprocal(rstd_h, rms_h))
            dve.wait_ge(consts, ALL_CONSTS)
            for t in range(NT):
                dve.wait_ge(logits_ps, t + 1)
                ins = dve.scalar_tensor_tensor(out=lg[:, t, :], in0=L[t][:, 0:NR],
                                               scalar=rstd_h[:, t:t + 1], in1=b_router[:, :],
                                               op0=ALU.mult, op1=ALU.add)
                ins.then_inc(r_step, 1)
                steps[0] += 1
            dve.wait_ge(r_step, steps[0])
            lg_g, lg_e = lg[:, :, 0:NGRP], lg[:, :, NGRP:NR]
            then_step(dve.tensor_reduce(g_max, lg_g, AX_X, ALU.max))
            dve.tensor_tensor(g_shifted, lg_g, bc(g_max, NGRP), ALU.subtract).then_inc(exp_in, 1)
            first_of(group_hot, lg_g, g_max, NGRP, g_scratch)
            then_step(dve.tensor_scalar(group_hot, group_hot, BIG, -BIG, ALU.mult, ALU.add))
            then_step(dve.tensor_tensor(masked.rearrange("p a (g e) -> p a g e", g=NGRP),
                                        lg_e.rearrange("p a (g e) -> p a g e", g=NGRP),
                                        group_hot.unsqueeze(3).to_broadcast([P, NT, NGRP, EPG]), ALU.add))
            then_step(dve.tensor_reduce(m1, masked, AX_X, ALU.max))
            first_of(hot1, masked, m1, NEXP, e_scratch)
            then_step(dve.scalar_tensor_tensor(out=masked2, in0=hot1, scalar=-2 * BIG, in1=masked,
                                               op0=ALU.mult, op1=ALU.add))
            then_step(dve.tensor_reduce(m2, masked2, AX_X, ALU.max))
            dve.tensor_tensor(d21, m2, m1, ALU.subtract).then_inc(exp_in, 1)
            first_of(hot2, masked2, m2, NEXP, e_scratch)
            dve.tensor_tensor(mask[:, :, :], hot1, hot2, ALU.add).then_inc(mask_done, 1)
            dve.wait_ge(exp_done, 2)
            then_step(dve.tensor_reduce(g_sum, g_exp, AX_X, ALU.add))
            then_step(dve.scalar_tensor_tensor(out=w1, in0=e21, scalar=1.0, in1=g_sum, op0=ALU.add, op1=ALU.mult))
            dve.reciprocal(w1, w1).then_inc(w1_done, 1)
            dve.wait_ge(mask_done, 1)
            then_step(dve.tensor_scalar(off, mask[:, :, :], -1000.0, 1000.0, ALU.mult, ALU.add))
            dve.wait_ge(ranks_ps, 1)
            dve.tensor_copy(count_i[:, :], R[:, COUNTS]).then_inc(counts_ready, 1)
            dve.tensor_copy(count_f[:, :], R[:, COUNTS]).then_inc(count_f_ready, 1)
            then_step(dve.tensor_tensor(rank_of[:, :, :], off, R[:, 0:NT * NEXP].rearrange("p (a e) -> p a e", a=NT),
                                        ALU.add))
            dve.wait_ge(count_f_ready, 1)

            def run_pass(s, n, q, e, g):
                iota = iota_cap
                if s is extra:
                    iota = iota_pass
                    dve.tensor_scalar(iota_pass[:, :], iota_pass[:, :], float(CAP), None, ALU.add
                                      ).then_inc(iota_moved, 1)
                    dve.wait_ge(iota_moved, n + 1)
                for t in range(NT):
                    ins = dve.tensor_scalar(sel[:, t, :], iota[:, :], rank_of[:, t, bass.ds(e, 1)], rstd_h[:, t:t + 1],
                                            ALU.is_equal, ALU.mult)
                ins.then_inc(s.sel, 1)
                dve.wait_ge(weights_ready, 1)
                for t in range(NT):
                    dst = scat[:, t, q * CAP:(q + 1) * CAP] if s is first else scat_x[:, t, :]
                    dve.tensor_scalar(dst, iota[:, :], rank_of[:, t, bass.ds(e, 1)], weight_of[:, t, bass.ds(e, 1)],
                                      ALU.is_equal, ALU.mult)
                dve.wait_ge(s.xeT_ps, n + 1)
                dve.tensor_tensor(xeT[:, :, :, :], TR[:, :].rearrange("p (b j c) -> p b j c", b=KC, j=NQ),
                                  g_ffn.rearrange("p (j b) -> p b j", b=KC).unsqueeze(3).to_broadcast([P, KC, NQ, CAP]),
                                  ALU.mult).then_inc(s.xeT, 1)
                dve.wait_ge(s.silu, n + 1)
                dve.tensor_tensor(hT[:, :, :], silu_g[:, :, :],
                                  TR[:, 0:256].rearrange("p (b c) -> p b c", b=2)[:, :, 2 * CAP:4 * CAP],
                                  ALU.mult).then_inc(s.hT, 1)

            def scatter(s, m):
                dve.wait_ge(acc_init, NT)
                for t in range(NT):
                    for j in range(NB):
                        dve.wait_ge(s.scattered, NT * NB * m + NB * t + j + 1)
                        cols = slice(j * NBLK, (j + 1) * NBLK)
                        dve.tensor_tensor(acc[:, t, cols], O[j][:, :], acc[:, t, cols], ALU.add).then_inc(s.o_free, 1)

            def first_ranks():
                dve.tensor_copy(iota_pass[:, :], iota_cap[:, :])
                dve.drain()

            def scale_out(t):
                dve.wait_ge(ssq_o_done, NB * (t + 1))
                dve.tensor_reduce(ssq_o[:, t:t + 1], sumsq_o[:, t, :], AX_X, ALU.add).then_inc(ssq_o_sum, 1)
                dve.wait_ge(rms_o_done, t + 1)
                dve.reciprocal(rstd_o[:, t:t + 1], rms_o[:, t:t + 1]).then_inc(rstd_o_done, 1)
                dve.wait_ge(rstd_o_done, t + 1)
                dve.wait_ge(acc_g_done, NB * (t + 1))
                dve.tensor_scalar(acc[:, t, 0:D // 2], h[:, t, 0:D // 2], rstd_o[:, t:t + 1], None, ALU.mult
                                  ).then_inc(out_ready, 1)

            def last_scatter(s, m):
                for t in range(NT):
                    for j in range(NB):
                        dve.wait_ge(s.scattered, NT * NB * m + NB * t + j + 1)
                        cols = slice(j * NBLK, (j + 1) * NBLK)
                        dve.tensor_tensor(acc[:, t, cols], O[j][:, :], acc[:, t, cols], ALU.add).then_inc(s.o_free, 1)
                        if t == j == 0:
                            dve.wait_ge(final_in, 16)
                            dve.wait_ge(first.xe_ps, NEXP)
                        dve.wait_ge(s.o_free, adds_done(m) + NB * t + j + 1)
                        dve.tensor_tensor(h[:, t, cols], acc[:, t, cols], g_final[:, cols], ALU.mult
                                          ).then_inc(acc_g_done, 1)
                        if t == 1 and j == 1:
                            scale_out(0)
                scale_out(1)

            experts(dve, run_pass, scatter, after_extra=lambda: dve.sem_inc(extras_over, 1),
                    before_extra=first_ranks, last_scatter=last_scatter)

        @block.tensor
        def _(pe):
            pe.wait_ge(consts, IDENT_READY)

            def transpose_x(k):
                pe.wait_ge(x_in[k * P // NBLK], 16)
                if k >= 4:
                    pe.wait_ge(xt_lo, k - 3)
                for t in range(NT):
                    ins = pe.transpose(X[k % 4][:, t * P:(t + 1) * P], h[:, t, k * P:(k + 1) * P], ident[:, :])
                ins.then_inc(xt_ps, 1)

            def column_block(n, parity, ready=None, midway=None):
                for hc in range(HC):
                    pe.wait_ge(lo_done, HC * n + hc + 1)
                    for j in range(2):
                        k = 2 * hc + j
                        if ready is not None:
                            ready(k)
                        for t in range(NT):
                            toks = slice(t * P, (t + 1) * P)
                            for part, (a, b) in enumerate(((xT_hi, w_hi), (xT_hi, w_lo), (xT_lo, w_hi))):
                                ins = pe.matmul(Z[parity][t][:, :], a[:, k, toks], b[:, hc % 2, j, :],
                                                start=(k == 0 and part == 0), stop=(k == KD - 1 and part == 2))
                    ins.then_inc(w_used, 1)
                    if midway is not None:
                        midway(hc)

            for k in range(4):
                transpose_x(k)
            pe.wait_ge(cols_in, 16 * 3)
            pe.transpose(Z[0][0][:, 0:2 * KD + GRP], col_rows[:, :], ident[0:2 * KD + GRP, 0:2 * KD + GRP]
                         ).then_inc(cols_ps, 1)
            pe.wait_ge(cols_done, 1)

            def next_x(hc):
                for k in (2 * hc + 4, 2 * hc + 5):
                    if k < KD:
                        transpose_x(k)

            column_block(0, 0, lambda k: pe.wait_ge(xt_lo, k + 1), next_x)
            column_block(1, 1)
            pe.wait_ge(ws_masked, 1)
            pe.wait_ge(xt_lo, KD)
            for i in range(GRP // 2):
                for j in range(2):
                    ins = pe.transpose(X[i][:, j * P:(j + 1) * P], ws_raw[:, 2 * i + j, :], ident[:, :])
                ins.then_inc(wst_ps, 1)
            with pe.Fori(1, NB // 2 + 1) as m:
                for i in range(2):
                    pe.wait_ge(v_ready, 2 * NT * m - NT + NT * i)
                    column_block(2 * m + i, i)
            def mix_v(i):
                g, t = i // NT * 2, i % NT
                if i == 0:
                    pe.wait_ge(wst_done, GRP // 2)
                pe.wait_ge(ln_done, i + 1)
                if i >= 4:
                    pe.wait_ge(sv_done, i - 3)
                for j in range(2):
                    ins = pe.matmul(X[i % 4][:, j * GD:(j + 1) * GD], ws_T[:, g + j, :],
                                    v[:, t, (g + j) * GD:(g + j + 1) * GD], start=True, stop=True)
                ins.then_inc(sv_ps, 1)

            pe.wait_ge(u_ready, NT)
            column_block(NB + 2, 0, midway=mix_v)

            def transpose_y(i):
                pe.wait_ge(y_done, NT * (i // 2 + 1))
                if i < 4:
                    pe.wait_ge(sv_done, NT * GRP // 2)
                else:
                    pe.wait_ge(yt_lo, i - 3)
                for j in range(2):
                    for t in range(NT):
                        ins = pe.transpose(X[i % 4][:, j * T + t * P:j * T + (t + 1) * P],
                                           v[:, t, (2 * i + j) * P:(2 * i + j + 1) * P], ident[:, :])
                ins.then_inc(yt_ps, 1)

            pe.wait_ge(u_ready, 2 * NT)
            column_block(NB + 3, 1, midway=lambda hc: transpose_y(hc) if hc < HC - 2 else None)

            def transpose_h(b):
                pe.wait_ge(h_done, NT * (b + 1))
                pe.wait_ge(yt_lo, KD // 2)
                if b:
                    pe.wait_ge(ht_act, b)
                    pe.wait_ge(ht_dve, b)
                for i in range(2):
                    for j in range(2):
                        k = 4 * b + 2 * i + j
                        for t in range(NT):
                            ins = pe.transpose(X[i][:, j * T + t * P:j * T + (t + 1) * P],
                                               h[:, t, k * P:(k + 1) * P], ident[:, :])
                    ins.then_inc(ht_ps, 1)

            def logits(b):
                if b == 0:
                    pe.wait_ge(router_w_ready, 1)
                pe.wait_ge(ht_act, b + 1)
                pe.wait_ge(ht_dve, b + 1)
                for t in range(NT):
                    for k in range(4 * b, 4 * b + 4):
                        ins = pe.matmul(L[t][:, 0:NR], h_T[:, k - 4 * b, t * P:(t + 1) * P], w_router[:, k, :],
                                        start=(k == 0), stop=(k == KD - 1))
                    if b == NB - 1:
                        ins.then_inc(logits_ps, 1)

            for b in range(NB):
                def midway(hc):
                    if b == 0 and hc in (1, 2):
                        transpose_y(HC - 2 + hc - 1)
                    if b and hc == 3:
                        transpose_h(b - 1)
                    if b and hc == 6:
                        logits(b - 1)

                if b < 2:
                    pe.wait_ge(u_ready, NT * (b + 3))
                else:
                    pe.wait_ge(h_done, NT * (b - 1))
                column_block(2 * NB + b, b % 2, (lambda k: pe.wait_ge(yt_lo, k // 2 + 1)) if b == 0 else None, midway)
            transpose_h(NB - 1)
            logits(NB - 1)
            pe.wait_ge(consts, ALL_CONSTS)
            pe.wait_ge(mask_done, 1)
            pe.matmul(R[:, 0:NEXP], before[:, :], mask[:, 0, :], start=True, stop=True)
            pe.matmul(R[:, NEXP:2 * NEXP], ones_bf[:, :], mask[:, 0, :], start=True, stop=False)
            pe.matmul(R[:, NEXP:2 * NEXP], before[:, :], mask[:, 1, :], start=False, stop=True)
            pe.matmul(R[:, COUNTS], ones_bf[:, :], mask[:, 0, :], start=True, stop=False)
            pe.matmul(R[:, COUNTS], ones_bf[:, :], mask[:, 1, :], start=False, stop=True).then_inc(ranks_ps, 1)

            def run_pass(s, n, q, e, g):
                is_first = s is first
                pe.wait_ge(s.sel, n + 1)
                for t in range(NT):
                    for j in range(NB):
                        ins = pe.matmul(XE[j * CAP:(j + 1) * CAP, :], sel[:, t, :],
                                        h[:, t, j * NBLK:(j + 1) * NBLK], start=(t == 0), stop=(t == NT - 1))
                ins.then_inc(s.xe_ps, 1)
                pe.wait_ge(s.xe, n + 1)
                for b in range(KC):
                    ins = pe.transpose(TR[:, b * P:(b + 1) * P], xe[:, b * P:(b + 1) * P], ident[:, :])
                ins.then_inc(s.xeT_ps, 1)
                pe.wait_ge(s.xeT, n + 1)
                for kc in range(FT):
                    if is_first:
                        wait_chunk(pe, 2 * kc, g, q)
                        wait_chunk(pe, 2 * kc + 1, g, q)
                    for kk in range(KC):
                        for c in range(NQ):
                            half = kk * FE + (c % 2) * 256
                            ins = pe.matmul(GU[c * CAP:(c + 1) * CAP, 0:256], xeT[:, kk, kc, :],
                                            slot_of(2 * kc + c // 2, q % 2)[:, half:half + 256],
                                            start=(kc == 0 and kk == 0), stop=(kc == FT - 1 and kk == KC - 1))
                    if is_first and kc < NSGL // 2:
                        ins.then_inc(chunk_used, 1)
                ins.then_inc(s.gu_ps, 1)
                if is_first and q == NQ - 1:
                    transpose_scat(first)
                pe.wait_ge(s.gu, n + 1)
                for b in range(2):
                    ins = pe.transpose(TR[:, b * P:(b + 1) * P], gu[:, b * P:(b + 1) * P], ident[:, :])
                ins.then_inc(s.tr_ps, 1)
                pe.wait_ge(s.hT, n + 1)
                for f in range(FT):
                    if is_first:
                        wait_chunk(pe, 8 + f, g, q)
                    for j in range(NB):
                        ins = pe.matmul(Y[j * CAP:(j + 1) * CAP, :], hT[:, f % 2, (f // 2) * CAP:(f // 2 + 1) * CAP],
                                        slot_of(8 + f, q % 2)[:, j * NBLK:(j + 1) * NBLK], start=(f == 0), stop=(f == FT - 1))
                ins.then_inc(s.y_ps, 1)
                if not is_first:
                    transpose_scat(extra)

            def transpose_scat(s):
                for t in range(NT):
                    if s is first:
                        ins = pe.transpose(XE[:, t * P:(t + 1) * P], scat[:, t, :], ident[:, :])
                    else:
                        ins = pe.transpose(XE[0:CAP, t * P:(t + 1) * P], scat_x[:, t, :], ident[:, :])
                ins.then_inc(s.scat_ps, 1)

            def scatter(s, m):
                a, b = (scatT, y) if s is first else (scatT_x, y_x)
                pe.wait_ge(s.scatT, m + 1)
                for t in range(NT):
                    for j in range(NB):
                        if t == 0:
                            pe.wait_ge(s.y, NB * (NQ * m + NQ - 1 if s is first else m) + j + 1)
                        pe.wait_ge(s.o_free, NT * NB * m + NB * t + j + 1)
                        pe.matmul(O[j][:, :], a[:, t, :], b[:, j * NBLK:(j + 1) * NBLK],
                                  start=True, stop=True).then_inc(s.scattered, 1)

            pe.wait_ge(counts_ready, 1)
            experts(pe, run_pass, scatter, at_start=lambda: pe.sem_inc(no_more_passes, 1),
                    after_extra=lambda: pe.sem_inc(no_more_passes, 1))


_INS = ["x", "norm_mix", "norm_ffn", "norm_final", "a_w_in", "a_ln_g", "a_ln_b", "a_w_s", "a_b_s", "a_w_out",
        "r_w_group", "r_b_group", "r_w_exp", "r_b_exp", "e_w_gate", "e_w_up", "e_w_down"]


def kernel(**inputs):
    import numpy as _np
    import concourse.bacc as _bacc
    from concourse.bass_utils import run_bass_kernel_spmd as _run

    nc = _bacc.Bacc("TRN2", target_bir_lowering=False, num_devices=1)
    arrays, args = {}, []
    for name in _INS:
        a = _np.ascontiguousarray(inputs[name])
        arrays[f"in_{name}"] = a
        args.append(nc.dram_tensor(f"in_{name}", a.shape, mybir.dt.from_np(a.dtype), kind="ExternalInput").ap())
    out = nc.dram_tensor("out_h", inputs["x"].shape, F32, kind="ExternalOutput").ap()
    hybrid_layer(nc, *args, out)
    r = _run(nc, [arrays], core_ids=[0])
    return r.results[0]["out_h"]
```
